# Optimizing a Trainium2 kernel written in Bass

```python
import jax, jax.numpy as jnp
from jax import lax
import numpy as np

D_MODEL = 1024
BATCH = 1
SEQ = 512
DEPTH = 2

N_MIXERS = 2
N_GLA = (DEPTH + 1) // 2
N_POOL = DEPTH // 2
EPS = 1e-6
D_FF = 2816
GLA_HEADS = 4
GLA_KD = D_MODEL // 2
GLA_VD = D_MODEL
GLA_DK = GLA_KD // GLA_HEADS
GLA_DV = GLA_VD // GLA_HEADS
GATE_RANK = 16
GATE_TAU = 16.0
CHUNK = 64
POOL_WINDOWS = (2, 4, 8, 16)
POOL_GROUPS = len(POOL_WINDOWS)
POOL_GC = D_MODEL // POOL_GROUPS
MEM_LEN = 256
X_HEADS = 4
X_DH = D_MODEL // X_HEADS

kernel_name = "hybrid_gla_pool_macaron_memxattn"

def rmsnorm(x, g):
    xf = x.astype(jnp.float32)
    y = xf * lax.rsqrt(jnp.mean(xf * xf, axis=-1, keepdims=True) + EPS)
    return (y * g.astype(jnp.float32)).astype(x.dtype)

def swiglu_ffn(h, w_gu, w_down):
    g, u = jnp.split(h @ w_gu, 2, axis=-1)
    return (jax.nn.silu(g) * u) @ w_down

def gla_mixer(h, w_in, w_g1, w_g2, b_g, g_onorm, w_out):
    B, S, _ = h.shape
    N = S // CHUNK
    f32 = jnp.float32
    proj = h @ w_in
    q, k, v, r = jnp.split(proj, [GLA_KD, 2 * GLA_KD, 2 * GLA_KD + GLA_VD], axis=-1)
    glog = jax.nn.log_sigmoid(((h @ w_g1) @ w_g2 + b_g).astype(f32)) / GATE_TAU

    def heads(t, dh):
        return t.reshape(B, N, CHUNK, GLA_HEADS, dh).transpose(0, 3, 1, 2, 4).astype(f32)

    q = heads(q, GLA_DK) * (GLA_DK ** -0.5)
    k = heads(k, GLA_DK)
    v = heads(v, GLA_DV)
    b = jnp.cumsum(heads(glog, GLA_DK), axis=3)
    b_last = b[:, :, :, -1:, :]
    b_ref = b[:, :, :, CHUNK // 2 - 1:CHUNK // 2, :]

    A = jnp.einsum('bhnik,bhnjk->bhnij', q * jnp.exp(b - b_ref), k * jnp.exp(b_ref - b))
    causal = jnp.tril(jnp.ones((CHUNK, CHUNK), dtype=bool))
    A = jnp.where(causal, A, 0.0)
    o_intra = jnp.einsum('bhnij,bhnjv->bhniv', A, v)

    q_in = q * jnp.exp(b)
    k_st = k * jnp.exp(b_last - b)
    decay = jnp.exp(b_last[:, :, :, 0, :])

    def step(state, xs):
        qn, kn, vn, dn = xs
        o = jnp.einsum('bhik,bhkv->bhiv', qn, state)
        state = dn[..., None] * state + jnp.einsum('bhjk,bhjv->bhkv', kn, vn)
        return state, o

    xs = tuple(jnp.moveaxis(t, 2, 0) for t in (q_in, k_st, v, decay))
    s0 = jnp.zeros((B, GLA_HEADS, GLA_DK, GLA_DV), f32)
    _, o_inter = lax.scan(step, s0, xs)
    o = o_intra + jnp.moveaxis(o_inter, 0, 2)
    o = o.transpose(0, 2, 3, 1, 4).reshape(B, S, GLA_HEADS, GLA_DV)
    o = rmsnorm(o, g_onorm).reshape(B, S, GLA_VD)
    o = (o * jax.nn.silu(r.astype(f32))).astype(h.dtype)
    return o @ w_out

def causal_window_mean(u, w):
    S = u.shape[1]
    cs = jnp.cumsum(u.astype(jnp.float32), axis=1)
    cs = jnp.pad(cs, ((0, 0), (1, 0), (0, 0)))
    upper = cs[:, 1:]
    lower = jnp.pad(cs, ((0, 0), (w - 1, 0), (0, 0)))[:, :S]
    count = jnp.minimum(jnp.arange(1, S + 1), w).astype(jnp.float32)
    return (upper - lower) / count[None, :, None]

def pool_mixer(h, w_grp, b_grp, scale):
    B, S, _ = h.shape
    groups = []
    for gi, w in enumerate(POOL_WINDOWS):
        u = h[..., gi * POOL_GC:(gi + 1) * POOL_GC]
        groups.append(causal_window_mean(u, w) - u.astype(jnp.float32))
    p = jnp.stack(groups, axis=2).astype(h.dtype)
    y = jnp.einsum('bsgc,gcd->bsgd', p, w_grp) + b_grp
    return y.reshape(B, S, D_MODEL) * scale

def mem_cross_attn(h, mem_n, w_q, w_kv, w_o):
    B, S, _ = h.shape
    q = (h @ w_q).reshape(B, S, X_HEADS, X_DH)
    k, v = jnp.split(mem_n @ w_kv, 2, axis=-1)
    k = k.reshape(B, MEM_LEN, X_HEADS, X_DH)
    v = v.reshape(B, MEM_LEN, X_HEADS, X_DH)
    s = jnp.einsum('bshd,bmhd->bhsm', q, k).astype(jnp.float32) * (X_DH ** -0.5)
    p = jax.nn.softmax(s, axis=-1).astype(h.dtype)
    o = jnp.einsum('bhsm,bmhd->bshd', p, v).reshape(B, S, D_MODEL)
    return o @ w_o

def setup_inputs(seed: int = 0) -> dict:
    key = jax.random.key(seed)
    ks = iter(jax.random.split(key, 40))

    def nrm(shape, fan_in):
        return jax.random.normal(next(ks), shape, jnp.float32) * (fan_in ** -0.5)

    def gain(shape):
        return 1.0 + 0.02 * jax.random.normal(next(ks), shape, jnp.float32)

    def small(shape):
        return 0.01 * jax.random.normal(next(ks), shape, jnp.float32)

    D = D_MODEL
    return {
        "x": jax.random.normal(next(ks), (BATCH, SEQ, D), jnp.float32),
        "mem": jax.random.normal(next(ks), (BATCH, MEM_LEN, D), jnp.float32),
        "n_ffn1": gain((DEPTH, D)),
        "ffn1_w_gu": nrm((DEPTH, D, 2 * D_FF), D),
        "ffn1_w_down": nrm((DEPTH, D_FF, D), D_FF),
        "n_mix": gain((DEPTH, D)),
        "gla_w_in": nrm((N_GLA, D, 2 * GLA_KD + 2 * GLA_VD), D),
        "gla_w_g1": nrm((N_GLA, D, GATE_RANK), D),
        "gla_w_g2": nrm((N_GLA, GATE_RANK, GLA_KD), GATE_RANK),
        "gla_b_g": small((N_GLA, GLA_KD)),
        "gla_onorm": gain((N_GLA, GLA_DV)),
        "gla_w_out": nrm((N_GLA, GLA_VD, D), GLA_VD),
        "pool_w": nrm((N_POOL, POOL_GROUPS, POOL_GC, POOL_GC), POOL_GC),
        "pool_b": small((N_POOL, POOL_GROUPS, POOL_GC)),
        "pool_scale": gain((N_POOL, D)),
        "n_xattn": gain((DEPTH, D)),
        "n_mem": gain((DEPTH, D)),
        "x_w_q": nrm((DEPTH, D, D), D),
        "x_w_kv": nrm((DEPTH, D, 2 * D), D),
        "x_w_o": nrm((DEPTH, D, D), D),
        "n_ffn2": gain((DEPTH, D)),
        "ffn2_w_gu": nrm((DEPTH, D, 2 * D_FF), D),
        "ffn2_w_down": nrm((DEPTH, D_FF, D), D_FF),
        "n_final": gain((D,)),
    }

def reference(x, mem, n_ffn1, ffn1_w_gu, ffn1_w_down, n_mix, gla_w_in, gla_w_g1,
              gla_w_g2, gla_b_g, gla_onorm, gla_w_out, pool_w, pool_b, pool_scale,
              n_xattn, n_mem, x_w_q, x_w_kv, x_w_o, n_ffn2, ffn2_w_gu, ffn2_w_down,
              n_final):
    for i in range(DEPTH):
        x = x + 0.5 * swiglu_ffn(rmsnorm(x, n_ffn1[i]), ffn1_w_gu[i], ffn1_w_down[i])
        h = rmsnorm(x, n_mix[i])
        j = i // N_MIXERS
        if i % N_MIXERS == 0:
            mix = gla_mixer(h, gla_w_in[j], gla_w_g1[j], gla_w_g2[j], gla_b_g[j],
                            gla_onorm[j], gla_w_out[j])
        else:
            mix = pool_mixer(h, pool_w[j], pool_b[j], pool_scale[j])
        x = x + mix
        x = x + mem_cross_attn(rmsnorm(x, n_xattn[i]), rmsnorm(mem, n_mem[i]),
                               x_w_q[i], x_w_kv[i], x_w_o[i])
        x = x + 0.5 * swiglu_ffn(rmsnorm(x, n_ffn2[i]), ffn2_w_gu[i], ffn2_w_down[i])
    return rmsnorm(x, n_final)


_drawn_inputs = setup_inputs


def setup_inputs(seed=0):
    import zlib

    import numpy as np

    out = dict(_drawn_inputs(seed))
    spreads = {}
    factors = {'n_ffn1': 4.032,
     'gla_b_g': 8.0,
     'gla_onorm': 5.109,
     'pool_b': 8.0,
     'pool_scale': 19.359,
     'n_xattn': 8.0,
     'n_mem': 8.0,
     'n_ffn2': 6.351,
     'n_final': 8.442}
    for name, (base, spread) in spreads.items():
        noise = np.random.default_rng([zlib.crc32(name.encode()), seed]).standard_normal(out[name].shape)
        drawn = base * np.exp(spread * noise) if base else spread * noise
        out[name] = __import__('jax').numpy.asarray(drawn.astype(out[name].dtype))
    for name, factor in factors.items():
        out[name] = (out[name] * factor).astype(out[name].dtype)
    return out
```

```python
from collections import namedtuple
from contextlib import ExitStack

import concourse.bass as bass
from concourse import mybir

F32 = mybir.dt.float32
F32R = mybir.dt.float32r
I32 = mybir.dt.int32
ALU = mybir.AluOpType
ACT = mybir.ActivationFunctionType
AX_X = mybir.AxisListType.X

P = 128
KB = 1024


def trunk(nc, io, out):
    _, SEQ, D = io.x.shape
    MEM = io.mem.shape[1]
    D_FF = io.ffn1_w_down.shape[1]
    T = SEQ // P
    C = D // P
    FC = D_FF // P
    HEADS = 4
    DK = D // 2 // HEADS
    DV = D // HEADS
    RANK = io.gla_w_g1.shape[2]
    TAU = 16.0
    CH = 64
    NCH = SEQ // CH
    DH = D // HEADS
    MT = MEM // P
    EPS = 1e-6
    WINDOWS = (2, 4, 8, 16)
    PAD = WINDOWS[-1]
    GROUPS = ((0, 8), (8, 8), (16, 6))
    COLS = 256
    assert (SEQ, D, DK, DV, MT, FC) == (512, 1024, P, 2 * P, 2, 22)

    at, slot_end, slot_rows = {}, [], []
    Place = namedtuple("Place", "slot part out")
    placed = {"parts": 0, "outs": 0}

    def place(name, parts, outs, rows=0):
        at[name] = Place(len(slot_end), placed["parts"], placed["outs"])
        placed["parts"] += parts
        placed["outs"] += outs
        if rows:
            slot_end.append(placed["parts"])
            slot_rows.append(rows)

    def place_ffn(n):
        for s in range(FC):
            place(("gu", n, s), 2, 2, C)
        for pair in range(C // 2):
            for g, (_, rows) in enumerate(GROUPS):
                place(("down", n, pair, g), 2, 2 if g == len(GROUPS) - 1 else 0, rows)

    def place_cross_keys(i):
        for pair in range(4):
            place(("xk", i, pair), 2, 2, C)

    def place_cross(i):
        for pair in range(4):
            place(("xq", i, pair), 2, 2, C)
        place(("xv", i, 0), 2, 2, C)
        for h in range(1, 4):
            place(("xv", i, h), 2, 2, C)
            place(("pv", i, h - 1), 2, 2)
        place(("pv", i, 3), 2, 2)
        for pair in range(4):
            place(("xo", i, pair), 2, 2, C)

    def place_gla():
        for name in ("Q0", "K0", "V0", "R0", "V1", "c0", "R1", "c1", "Q1", "K1", "V2", "OUT0", "R2", "c2", "V3", "R3", "c3"):
            if name[0] == "c":
                place(name, 2, 2)
            elif name == "OUT0":
                for pair in range(4):
                    place(("OUT", 0, pair), 2, 2, 4)
            else:
                place(name, *((4, 4) if name[0] == "V" else (2, 2)), C)
        place_cross_keys(0)
        for pair in range(4):
            place(("OUT", 1, pair), 2, 2, 4)
        place_cross(0)

    def place_rest():
        place_ffn(1)
        place_ffn(2)
        place_cross_keys(1)
        place("pool", 8, 8, C)
        place_cross(1)
        place_ffn(3)

    for m in range(C):
        place(("in", m), 1, 1)
    place_ffn(0)
    place_gla()
    place_rest()
    SLOTS = len(slot_end)

    OUTS = placed["outs"]

    LAST = 8
    H_BASE = {0: 0, 1: 8, 2: 16, 3: 24, 4: 32, 6: 40, 7: 48}

    ctx = ExitStack()
    with ctx:
        def sb(name, shape, dt=F32):
            return ctx.enter_context(nc.sbuf_tensor(name, shape, dt))

        def sem(name):
            return ctx.enter_context(nc.semaphore(name))

        x = sb("x", [P, C, SEQ])
        h_hi, h_lo = sb("h_hi", [P, C, SEQ], F32R), sb("h_lo", [P, C, SEQ], F32R)
        raw = sb("raw", [P, 2, C, COLS])
        w_hi, w_lo = sb("w_hi", [P, 2, C, COLS], F32R), sb("w_lo", [P, 2, C, COLS], F32R)
        rms = sb("rms", [P, SEQ])
        rms_tok = sb("rms_tok", [P, T])
        acc = sb("acc", [P, SEQ])
        t = sb("t", [P, 2, SEQ])
        sq = sb("sq", [P, 2, SEQ])
        ident, ones, mask = sb("ident", [P, P]), sb("ones", [P, P]), sb("mask", [P, P])
        eps = sb("eps", [P, 1])
        decay = sb("decay", [P, NCH])
        inv_count = sb("inv_count", [P, 4, PAD])
        smax, sbias, ssum = sb("smax", [P, T]), sb("sbias", [P, T]), sb("ssum", [P, T])
        mem_rms = sb("mem_rms", [P, MT])

        rows, at_row = [], {}
        for name, vec in (("n_ffn1", io.n_ffn1), ("n_mix", io.n_mix), ("n_xattn", io.n_xattn), ("n_mem", io.n_mem),
                          ("n_ffn2", io.n_ffn2), ("n_final", io.n_final), ("pool_scale", io.pool_scale),
                          ("pool_b", io.pool_b), ("gla_b_g", io.gla_b_g), ("gla_onorm", io.gla_onorm)):
            flat = {1: "(r p) -> r p", 2: "l (r p) -> (l r) p", 3: "l g (r p) -> (l g r) p"}[len(vec.shape)]
            at_row[name] = sum(r.shape[0] for r in rows)
            rows.append(vec.rearrange(flat, p=P))
        NR = sum(r.shape[0] for r in rows)
        cols = sb("cols", [P, NR])

        def col(name, c):
            return cols[:, at_row[name] + c:at_row[name] + c + 1]

        def gain(f, c):
            name, layer = (("n_ffn1", 0), ("n_mix", 0), ("n_xattn", 0), ("n_ffn2", 0), ("n_ffn1", 1), ("n_mix", 1),
                           ("n_xattn", 1), ("n_ffn2", 1), ("n_final", 0))[f]
            return col(name, layer * C + c)

        def region(name, offset, shape, dt=F32):
            with ExitStack() as e:
                if offset:
                    e.enter_context(nc.sbuf_tensor(f"below_{name}", [P, offset // 4], F32))
                return e.enter_context(nc.sbuf_tensor(name, shape, dt))

        x_tok = region("x_tok", 0, [P, T, D])
        vec_rows = region("vec_rows", 16 * KB, [P, P])
        mid_hi = region("mid_hi", 0, [P, FC, SEQ], F32R)
        mid_lo = region("mid_lo", 44 * KB, [P, FC, SEQ], F32R)
        o_hi, o_lo = region("o_hi", 0, [P, 4, SEQ], F32R), region("o_lo", 8 * KB, [P, 4, SEQ], F32R)
        u = region("u", 16 * KB, [P, 2, SEQ])
        b = region("b", 20 * KB, [P, HEADS, SEQ])
        q, k = region("q", 28 * KB, [P, 2, SEQ]), region("k", 32 * KB, [P, 2, SEQ])
        v_hi, v_lo = region("v_hi", 36 * KB, [P, 2, T, DV], F32R), region("v_lo", 44 * KB, [P, 2, T, DV], F32R)
        S = region("S", 52 * KB, [P, 2, DV])
        S_hi, S_lo = region("S_hi", 54 * KB, [P, 7, DV], F32R), region("S_lo", 61 * KB, [P, 7, DV], F32R)
        g1 = region("g1", 52 * KB, [P, C, RANK])
        g1_hi = region("g1_hi", 52 * KB + 512, [P, C, RANK], F32R)
        g1_lo = region("g1_lo", 53 * KB, [P, C, RANK], F32R)
        g2 = region("g2", 54 * KB, [RANK, HEADS * DK])
        g2_hi = region("g2_hi", 56 * KB, [RANK, HEADS * DK], F32R)
        g2_lo = region("g2_lo", 58 * KB, [RANK, HEADS * DK], F32R)
        gt = region("gt", 60 * KB, [RANK, SEQ])
        gt_hi = region("gt_hi", 62 * KB, [RANK, SEQ], F32R)
        gt_lo = region("gt_lo", 64 * KB, [RANK, SEQ], F32R)
        qk_hi, qk_lo = region("qk_hi", 68 * KB, [P, 2, SEQ], F32R), region("qk_lo", 72 * KB, [P, 2, SEQ], F32R)
        qin_hi, qin_lo = region("qin_hi", 76 * KB, [P, SEQ], F32R), region("qin_lo", 78 * KB, [P, SEQ], F32R)
        kst_hi, kst_lo = region("kst_hi", 80 * KB, [P, T, DK], F32R), region("kst_lo", 82 * KB, [P, T, DK], F32R)
        am_hi, am_lo = region("am_hi", 84 * KB, [P, T, P], F32R), region("am_lo", 86 * KB, [P, T, P], F32R)
        e = region("e", 88 * KB, [P, 2, SEQ])
        mem_tok = (region("mem_tok0", 20 * KB, [P, MT, D]), region("mem_tok1", 88 * KB, [P, MT, D]))
        p_tok = region("p_tok", 0, [P, HEADS, T, MEM])
        pT_hi, pT_lo = region("pT_hi", 16 * KB, [P, MT, SEQ], F32R), region("pT_lo", 20 * KB, [P, MT, SEQ], F32R)
        xv_hi, xv_lo = region("xv_hi", 24 * KB, [P, MT, D], F32R), region("xv_lo", 32 * KB, [P, MT, D], F32R)
        m_hi, m_lo = region("m_hi", 40 * KB, [P, C, MEM], F32R), region("m_lo", 48 * KB, [P, C, MEM], F32R)
        pT3_hi, pT3_lo = region("pT3_hi", 40 * KB, [P, MT, SEQ], F32R), region("pT3_lo", 44 * KB, [P, MT, SEQ], F32R)
        xk_hi, xk_lo = region("xk_hi", 56 * KB, [P, C, MEM], F32R), region("xk_lo", 64 * KB, [P, C, MEM], F32R)
        xq_hi, xq_lo = region("xq_hi", 72 * KB, [P, 4, SEQ], F32R), region("xq_lo", 80 * KB, [P, 4, SEQ], F32R)
        xo_hi, xo_lo = region("xo_hi", 56 * KB, [P, C, SEQ], F32R), region("xo_lo", 72 * KB, [P, C, SEQ], F32R)
        up = region("up", 0, [P, C, PAD + SEQ])
        sums = region("sums", 17 * KB, [P, 2, 2, PAD + SEQ])
        p_hi, p_lo = region("p_hi", 72 * KB, [P, 4, SEQ], F32R), region("p_lo", 80 * KB, [P, 4, SEQ], F32R)
        y_tok = region("y_tok", 0, [P, T, D])

        ps = ctx.enter_context(nc.psum_tensor("ps", [P, 8, 512], F32))

        names = """vec_loaded gates_loaded identity_ready consts_ready mask_ready cols_done cols_ready
                w_hi_ready w_lo_ready part_done evacuated x_ready h_hi_ready h_ready sq_ready sq_added
                norm_summed norm_root norm_ready silu_done mid_hi_ready mid_ready
                g_hi_ready g_lo_ready g1_done gt_ready gt_hi_ready gt_lo_ready z_done z_biased gate_neg gate_exp
                gate_ln gate_log b_ready scanmask_ready diff_ready exp_ready qk_scaled qk_hi_ready qk_lo_ready
                last_diff last_exp kst_ready in_exp decay_ready qin_ready qin_hi_ready qin_lo_ready a_done
                kst_hi_ready kst_lo_ready at_zeroed at_ready at_hi_ready at_lo_ready kv_done s_ready s_hi_ready
                s_lo_ready v_hi_ready r_silu o_squared o_summed o_root o_rms o_scaled o_hi_ready o_lo_ready
                half_added mem_loaded mem_squared mem_root mem_rms_ready mem_scaled mem_transposed m_hi_ready
                m_lo_ready xk_hi_ready xv_hi_ready xq_hi_ready scores_done max_ready neg_max_ready exp_done
                sum_inverted p_ready p_transposed pT_hi_ready pT_lo_ready xo_hi_ready
                pads_zeroed counts_ready up_ready window_ready mean_ready p_hi_ready p_lo_ready pool_biased
                y_ready y_transposed y_out_by_dve y_out_by_act stored
                tok_root tok_inverse tok_ready"""
        sig = namedtuple("Semaphores", names)(*[sem(name) for name in names.split()])
        raw_loaded = [sem("raw_loaded_even"), sem("raw_loaded_odd")]
        x_loaded = [sem(f"x_loaded{g}") for g in range(4)]

        block = ctx.enter_context(nc.Block())

        FEED_AFTER = (1, 4, 5, 8)
        X_COUNTED = (1, 4, 5, 6, 8)
        X_OUT = {0: ("in", 0), 2: ("OUT", 1, 0), 3: ("xo", 0, 0), 7: ("xo", 1, 0)}

        def x_final(f, m):
            if f in X_OUT:
                return sig.evacuated, at[X_OUT[f]].out + m + 1
            return sig.x_ready, C * X_COUNTED.index(f) + m + 1

        RMS_FEEDS = (0, 1, 3, 4, 5, 7)
        TOK_FEEDS = (1, 2, 6, LAST)
        UPDATE_ORDER = (0, 2, 1, 3, 4, 6, 5)
        UPDATES_BEFORE = (2, 4, 4, 4, 6, 7, 7)
        OUT_BANK = (4, 6, 7, 0, 1, 2, 3, 4)

        def three_products(out_ap, left, right, first, last):
            nc.tensor.matmul(out_ap, left[0], right[0], start=first, stop=False)
            nc.tensor.matmul(out_ap, left[0], right[1], start=False, stop=False)
            return nc.tensor.matmul(out_ap, left[1], right[0], start=False, stop=last)

        @block.sync
        def _(sp):
            for g in range(4):
                sp.dma_start(x_tok[:, :, g * COLS:(g + 1) * COLS],
                             io.x[0].rearrange("(t p) d -> p t d", p=P)[:, :, g * COLS:(g + 1) * COLS])\
                  .then_inc(x_loaded[g], 16)

            def load(w, split_before, nrows, src):
                if split_before is not None:
                    sp.wait_ge(sig.w_lo_ready, split_before)
                sp.dma_start(raw[:, w % 2, 0:nrows, :], src).then_inc(raw_loaded[w % 2], 16)

            def columns(weight, first_row, nrows, first_col):
                view = weight.rearrange("(k p) n -> p k n", p=P)
                return view[:, first_row:first_row + nrows, bass.ds(first_col, COLS)]

            def load_fixed(name, weight, first_row, nrows, first_col):
                w = at[name].slot
                load(w, w - 1 if w >= 2 else None, nrows, columns(weight, first_row, nrows, first_col))

            def load_ffn(n):
                layer = n // 2
                gu, down = ((io.ffn1_w_gu, io.ffn1_w_down), (io.ffn2_w_gu, io.ffn2_w_down))[n % 2]
                w0 = at[("gu", n, 0)].slot
                first = 0
                if n == 0:
                    load_fixed(("gu", 0, 0), gu[layer], 0, C, 0)
                    load_fixed(("gu", 0, 1), gu[layer], 0, C, D_FF)
                    first = 1
                with sp.Fori(first, FC // 2) as j:
                    load(w0, w0 - 1 + 2 * j, C, columns(gu[layer], 0, C, j * COLS))
                    load(w0 + 1, w0 + 2 * j, C, columns(gu[layer], 0, C, j * COLS + D_FF))
                w0 = at[("down", n, 0, 0)].slot
                with sp.Fori(0, 2) as i:
                    for pair in range(2):
                        for g, (row, nrows) in enumerate(GROUPS):
                            s = 3 * pair + g
                            load(w0 + s, w0 + s - 1 + 6 * i, nrows,
                                 columns(down[layer], row, nrows, i * (2 * COLS) + pair * COLS))

            def load_cross_keys(i):
                for pair in range(4):
                    load_fixed(("xk", i, pair), io.x_w_kv[i], 0, C, pair * COLS)

            def load_cross(i):
                for pair in range(4):
                    load_fixed(("xq", i, pair), io.x_w_q[i], 0, C, pair * COLS)
                for h in range(4):
                    load_fixed(("xv", i, h), io.x_w_kv[i], 0, C, D + h * COLS)
                for pair in range(4):
                    load_fixed(("xo", i, pair), io.x_w_o[i], 0, C, pair * COLS)

            load_ffn(0)
            for name in ("Q0", "K0", "V0", "R0", "V1", "R1", "Q1", "K1", "V2", "OUT0", "R2", "V3", "R3"):
                if name == "OUT0":
                    for pair in range(4):
                        load_fixed(("OUT", 0, pair), io.gla_w_out[0], 0, 4, pair * COLS)
                else:
                    first = {"Q": 0, "K": D // 2, "V": D, "R": 2 * D}[name[0]]
                    load_fixed(name, io.gla_w_in[0], 0, C, first + int(name[1]) * COLS)
            load_cross_keys(0)
            for pair in range(4):
                load_fixed(("OUT", 1, pair), io.gla_w_out[0], 4, 4, pair * COLS)
            load_cross(0)
            load_ffn(1)
            load_ffn(2)
            load_cross_keys(1)
            w = at["pool"].slot
            load(w, w - 1, C, io.pool_w[0].rearrange("g (k p) n -> p (g k) n", p=P))
            load_cross(1)
            load_ffn(3)
            for piece in range(2 * T):
                tile, half = piece % T, piece // T
                sp.wait_ge((sig.y_out_by_dve, sig.y_out_by_act)[piece % 2], piece // 2 + 1)
                sp.dma_start(out[0].rearrange("(t p) d -> p t d", p=P)[:, tile, half * 512:(half + 1) * 512],
                             y_tok[:, tile, half * 512:(half + 1) * 512]).then_inc(sig.stored, 16)
            sp.wait_ge(sig.stored, 2 * T * 16)

        @block.gpsimd
        def _(pool):
            row = 0
            for vec in rows:
                pool.dma_start(vec_rows[row:row + vec.shape[0], :], vec).then_inc(sig.vec_loaded, 16)
                row += vec.shape[0]
            nc.gpsimd.memset(ident[:], 0.0).then_inc(sig.consts_ready, 1)
            nc.gpsimd.memset(mask[:], 1.0).then_inc(sig.consts_ready, 1)
            nc.gpsimd.memset(ones[:], 1.0).then_inc(sig.consts_ready, 1)
            nc.gpsimd.memset(eps[:], EPS).then_inc(sig.consts_ready, 1)
            pool.wait_ge(sig.consts_ready, 4)
            nc.gpsimd.affine_select(out=ident[:], in_=ident[:], compare_op=ALU.not_equal, fill=1.0, base=0,
                                    pattern=[[-1, P]], channel_multiplier=1).then_inc(sig.identity_ready, 1)
            nc.gpsimd.affine_select(out=mask[:], in_=mask[:], compare_op=ALU.is_ge, fill=0.0, base=0,
                                    pattern=[[1, P]], channel_multiplier=-1).then_inc(sig.mask_ready, 1)
            pool.wait_ge(sig.mask_ready, 1)
            nc.gpsimd.memset(mask[0:CH, CH:P], 0.0).then_inc(sig.mask_ready, 1)

            def add_squares(f):
                for m in range(C):
                    pool.wait_ge(sig.sq_ready, C * f + m + 1)
                    if m == 0:
                        if f > 0:
                            pool.wait_ge(sig.norm_summed, f)
                        if f == 2:
                            pool.wait_ge(sig.at_lo_ready, HEADS)
                        nc.gpsimd.tensor_copy(acc[:], sq[:, 0, :]).then_inc(sig.sq_added, 1)
                    else:
                        pool.wait_ge(sig.sq_added, C * f + m)
                        nc.gpsimd.tensor_tensor(acc[:], acc[:], sq[:, m % 2, :], ALU.add).then_inc(sig.sq_added, 1)

            add_squares(0)
            add_squares(1)
            pool.wait_ge(sig.part_done, at["Q0"].part)
            pool.dma_start(g1[:], io.gla_w_g1[0].rearrange("(k p) r -> p k r", p=P)).then_inc(sig.gates_loaded, 16)
            pool.dma_start(g2[:], io.gla_w_g2[0]).then_inc(sig.gates_loaded, 16)
            pool.wait_ge(sig.norm_summed, 2)
            nc.gpsimd.memset(acc[:], 1.0).then_inc(sig.scanmask_ready, 1)
            pool.wait_ge(sig.scanmask_ready, 1)
            nc.gpsimd.memset(acc[:].rearrange("p (n c) -> p n c", c=CH)[:, :, 0:1], 0.0)\
              .then_inc(sig.scanmask_ready, 1)
            pool.wait_ge(sig.qin_ready, HEADS)
            pool.wait_ge(sig.decay_ready, HEADS)
            pool.dma_start(mem_tok[0][:], io.mem[0].rearrange("(t p) d -> p t d", p=P)).then_inc(sig.mem_loaded, 16)
            for f in (2, 3):
                add_squares(f)
            pool.wait_ge(sig.part_done, at[("gu", 1, 0)].part)
            pool.dma_start(mem_tok[1][:], io.mem[0].rearrange("(t p) d -> p t d", p=P)).then_inc(sig.mem_loaded, 16)
            for f in (4, 5, 6, 7, 8):
                add_squares(f)

        @block.tensor
        def _(pe):
            def chunk_bank(o):
                if o >= 4:
                    pe.wait_ge(sig.evacuated, o - 3)
                return o % 4

            def weights(s, kk, c):
                cs = slice(c * P, (c + 1) * P)
                return w_hi[:, s, kk, cs], w_lo[:, s, kk, cs]

            def project(name, right, nrows=C, k0=0, feed=None, n=SEQ):
                w = at[name].slot
                pe.wait_ge(sig.w_lo_ready, w + 1)
                for c in range(2):
                    bank = chunk_bank(at[name].out + c)
                    for kk in range(nrows):
                        if feed is not None and c == 0:
                            pe.wait_ge(sig.h_ready, H_BASE[feed] + kk + 1)
                        last = three_products(ps[:, bank, 0:n], weights(w % 2, kk, c),
                                              (right[0][:, k0 + kk, :], right[1][:, k0 + kk, :]),
                                              kk == 0, kk == nrows - 1)
                    last.then_inc(sig.part_done, 1)
                    if feed is not None and c == 0:
                        norm(feed)

            def project_rows(name, left, tiles, need=None):
                w = at[name].slot
                pe.wait_ge(sig.w_lo_ready, w + 1)
                for tt in range(tiles):
                    bank = chunk_bank(at[name].out + tt)
                    ts = slice(tt * P, (tt + 1) * P)
                    for kk in range(C):
                        last = three_products(ps[:, bank, 0:COLS], (left[0][:, kk, ts], left[1][:, kk, ts]),
                                              (w_hi[:, w % 2, kk, :], w_lo[:, w % 2, kk, :]), kk == 0, kk == C - 1)
                    last.then_inc(sig.part_done, 1)

            def norm(f):
                pe.wait_ge(sig.sq_added, C * (f + 1))
                pe.wait_ge(sig.consts_ready, 4)
                last = None
                if f in RMS_FEEDS:
                    last = nc.tensor.matmul(ps[:, 4, :], ones[:], acc[:], start=True, stop=True)
                if f in TOK_FEEDS:
                    for tt in range(T):
                        last = nc.tensor.matmul(ps[:, 5, tt:tt + 1], acc[:, tt * P:(tt + 1) * P], ones[:, 0:1],
                                                start=True, stop=True)
                last.then_inc(sig.norm_summed, 1)

            def ffn(n, between=None):
                hh = (h_hi, h_lo)
                for s in range(2):
                    project(("gu", n, s), hh, feed=(0, 3, 4, 7)[n] if s == 0 else None)
                w0, o0 = at[("gu", n, 0)].slot, at[("gu", n, 0)].out
                with pe.Fori(1, FC // 2) as j:
                    for s in range(2):
                        pe.wait_ge(sig.w_lo_ready, w0 + s + 1 + 2 * j)
                        for c in range(2):
                            o = o0 + 2 * s + c
                            pe.wait_ge(sig.evacuated, o - 3 + 4 * j)
                            for kk in range(C):
                                last = three_products(ps[:, o % 4, :], weights((w0 + s) % 2, kk, c),
                                                      (h_hi[:, kk, :], h_lo[:, kk, :]), kk == 0, kk == C - 1)
                            last.then_inc(sig.part_done, 1)
                if between is not None:
                    between()
                w0, o0 = at[("down", n, 0, 0)].slot, at[("down", n, 0, 0)].out
                with pe.Fori(0, 2) as i:
                    for pair in range(2):
                        for g, (k0, nrows) in enumerate(GROUPS):
                            s = 3 * pair + g
                            pe.wait_ge(sig.w_lo_ready, w0 + s + 1 + 6 * i)
                            pe.wait_ge(sig.mid_ready, FC * n + k0 + nrows)
                            for c in range(2):
                                o = o0 + 2 * pair + c
                                if g == 0:
                                    pe.wait_ge(sig.evacuated, o - 3 + 4 * i)
                                for kk in range(nrows):
                                    last = three_products(ps[:, o % 4, :], weights((w0 + s) % 2, kk, c),
                                                          (mid_hi[:, k0 + kk, :], mid_lo[:, k0 + kk, :]),
                                                          k0 + kk == 0, k0 + kk == FC - 1)
                                last.then_inc(sig.part_done, 1)

            pe.wait_ge(sig.identity_ready, 1)
            pe.wait_ge(sig.vec_loaded, 16 * len(rows))
            nc.tensor.transpose(ps[:, 7, 0:NR], vec_rows[0:NR, :], ident[0:NR, 0:NR]).then_inc(sig.cols_done, 1)
            for m in range(C):
                if m % 2 == 0:
                    pe.wait_ge(x_loaded[m // 2], 16)
                bank = chunk_bank(m)
                for tt in range(T):
                    last = nc.tensor.transpose(ps[:, bank, tt * P:(tt + 1) * P], x_tok[:, tt, m * P:(m + 1) * P], ident[:])
                last.then_inc(sig.part_done, 1)

            def gla_scores(h):
                pe.wait_ge(sig.kst_ready, h + 1)
                if h == 0:
                    pe.wait_ge(sig.z_biased, HEADS)
                else:
                    pe.wait_ge(sig.s_ready, 7 * h)
                if h >= 2:
                    pe.wait_ge(sig.o_root, h)
                for tt in range(T):
                    ts = slice(tt * P, (tt + 1) * P)
                    nc.tensor.transpose(ps[:, 4, ts], k[:, h % 2, ts], ident[:])
                pe.wait_ge(sig.qk_lo_ready, h + 1)
                for tt in range(T):
                    ts = slice(tt * P, (tt + 1) * P)
                    last = three_products(ps[:, 5, ts], (qk_hi[:, 1, ts], qk_lo[:, 1, ts]),
                                          (qk_hi[:, 0, ts], qk_lo[:, 0, ts]), True, True)
                last.then_inc(sig.a_done, 1)

            def gla_updates(h):
                pe.wait_ge(sig.kst_lo_ready, h + 1)
                pe.wait_ge(sig.at_ready, h + 1)
                pe.wait_ge(sig.evacuated, at[f"V{h}"].out + T)
                for n in UPDATE_ORDER:
                    tt, half = n // 2, n % 2
                    rs = slice(half * CH, (half + 1) * CH)
                    bank, cs = 4 + 2 * half + tt // 2, slice((tt % 2) * DV, (tt % 2 + 1) * DV)
                    three_products(ps[:, bank, cs], (kst_hi[rs, tt, :], kst_lo[rs, tt, :]),
                                   (v_hi[rs, h % 2, tt, :], v_lo[rs, h % 2, tt, :]), True, True)\
                        .then_inc(sig.kv_done, 1)

            def gla_outputs(h):
                pe.wait_ge(sig.at_lo_ready, h + 1)
                pe.wait_ge(sig.qin_lo_ready, h + 1)
                for c in range(2):
                    bank = chunk_bank(at[f"c{h}"].out + c)
                    vs = slice(c * P, (c + 1) * P)
                    for tt in range(T):
                        ts = slice(tt * P, (tt + 1) * P)
                        last = three_products(ps[:, bank, ts], (v_hi[:, h % 2, tt, vs], v_lo[:, h % 2, tt, vs]),
                                              (am_hi[:, tt, :], am_lo[:, tt, :]), True, False)
                        for n in (2 * tt, 2 * tt + 1):
                            if n == 0:
                                continue
                            pe.wait_ge(sig.s_lo_ready, 7 * h + n)
                            ns = slice(n * CH, (n + 1) * CH)
                            last = three_products(ps[:, bank, ns], (S_hi[:, n - 1, vs], S_lo[:, n - 1, vs]),
                                                  (qin_hi[:, ns], qin_lo[:, ns]), False, n % 2 == 1)
                    last.then_inc(sig.part_done, 1)

            def gla_norm(h):
                pe.wait_ge(sig.o_squared, 2 * h + 2)
                pe.wait_ge(sig.s_ready, 7 * (2, 2, 3, 4)[h])
                if h > 0:
                    pe.wait_ge(sig.o_root, h)
                for c in range(2):
                    last = nc.tensor.matmul(ps[:, 4, :], ones[:], sq[:, c, :], start=c == 0, stop=c == 1)
                last.then_inc(sig.o_summed, 1)

            def transpose_memory(i):
                pe.wait_ge(sig.mem_scaled, MT * (i + 1))
                if i == 0:
                    pe.wait_ge(sig.s_ready, 7 * HEADS)
                    pe.wait_ge(sig.o_root, HEADS - 1)
                else:
                    pe.wait_ge(sig.norm_root, RMS_FEEDS.index(4) + 1)
                for c in range(C):
                    for mt in range(MT):
                        cs = slice((c % 2) * MEM + mt * P, (c % 2) * MEM + (mt + 1) * P)
                        last = nc.tensor.transpose(ps[:, 4 + c // 2, cs], mem_tok[i][:, mt, c * P:(c + 1) * P], ident[:])
                    last.then_inc(sig.mem_transposed, 1)

            def cross_keys(i, pairs):
                for pair in pairs:
                    if pair == 0:
                        pe.wait_ge(sig.m_lo_ready, C * (i + 1))
                    project(("xk", i, pair), (m_hi, m_lo), n=MEM)

            def scores(i, h):
                n = HEADS * i + h
                pe.wait_ge(sig.evacuated, at[("xq", i, h)].out + 2)
                if h >= 2:
                    pe.wait_ge(sig.exp_done, T * (n - 1))
                else:
                    pe.wait_ge(sig.tok_ready, TOK_FEEDS.index(4 * i + 2) + 1)
                    pe.wait_ge(sig.m_lo_ready, C * (i + 1))
                for tt in range(T):
                    ts = slice(tt * P, (tt + 1) * P)
                    out_ap = ps[:, 4 + 2 * (h % 2) + tt // 2, (tt % 2) * MEM:(tt % 2 + 1) * MEM]
                    for d in range(2):
                        last = three_products(out_ap, (xq_hi[:, 2 * (h % 2) + d, ts], xq_lo[:, 2 * (h % 2) + d, ts]),
                                              (xk_hi[:, 2 * h + d, :], xk_lo[:, 2 * h + d, :]), d == 0, d == 1)
                last.then_inc(sig.scores_done, 1)

            def transpose_p(i, h):
                n = HEADS * i + h
                pe.wait_ge(sig.p_ready, n + 1)
                if h >= 2:
                    pe.wait_ge(sig.pT_lo_ready, n - 1)
                else:
                    pe.wait_ge(sig.exp_done, T * (HEADS * i + 3 + h))
                for mt in range(MT):
                    for tt in range(T):
                        last = nc.tensor.transpose(ps[:, 4 + 2 * (h % 2) + mt, tt * P:(tt + 1) * P],
                                                   p_tok[:, h, tt, mt * P:(mt + 1) * P], ident[:])
                last.then_inc(sig.p_transposed, 1)

            def weighted_values(i, h):
                n = HEADS * i + h
                pe.wait_ge(sig.pT_lo_ready, n + 1)
                right = (pT3_hi, pT3_lo) if h == 3 else (pT_hi, pT_lo)
                pe.wait_ge(sig.evacuated, at[("xv", i, h)].out + 2)
                for c in range(2):
                    bank = chunk_bank(at[("pv", i, h)].out + c)
                    vs = slice(h * DH + c * P, h * DH + (c + 1) * P)
                    for mt in range(MT):
                        last = three_products(ps[:, bank, :], (xv_hi[:, mt, vs], xv_lo[:, mt, vs]),
                                              (right[0][:, mt, :], right[1][:, mt, :]), mt == 0, mt == MT - 1)
                    last.then_inc(sig.part_done, 1)

            def cross(i):
                hh, mm = (h_hi, h_lo), (m_hi, m_lo)
                project(("xq", i, 0), hh, feed=4 * i + 2)
                for h in range(1, 4):
                    project(("xq", i, h), hh)
                    scores(i, h - 1)
                project_rows(("xv", i, 0), mm, MT)
                scores(i, 3)
                transpose_p(i, 0)
                for h in range(1, 4):
                    project_rows(("xv", i, h), mm, MT)
                    if h == 3:
                        transpose_p(i, h)
                    weighted_values(i, h - 1)
                    if h < 3:
                        transpose_p(i, h)
                weighted_values(i, 3)
                for pair in range(4):
                    project_cross_out(i, pair)

            def project_cross_out(i, pair):
                name = ("xo", i, pair)
                w = at[name].slot
                pe.wait_ge(sig.w_lo_ready, w + 1)
                for c in range(2):
                    bank = chunk_bank(at[name].out + c)
                    for kk in range(C):
                        if pair == 0 and c == 0 and kk % 2 == 0:
                            pe.wait_ge(sig.evacuated, at[("pv", i, kk // 2)].out + 2)
                        last = three_products(ps[:, bank, :], weights(w % 2, kk, c), (xo_hi[:, kk, :], xo_lo[:, kk, :]),
                                              kk == 0, kk == C - 1)
                    last.then_inc(sig.part_done, 1)

            ffn(0)
            hh, oo = (h_hi, h_lo), (o_hi, o_lo)
            project("Q0", hh, feed=1)
            pe.wait_ge(sig.g_lo_ready, 1)
            for kk in range(C):
                last = three_products(ps[0:RANK, 6, :], (g1_hi[:, kk, :], g1_lo[:, kk, :]),
                                      (h_hi[:, kk, :], h_lo[:, kk, :]), kk == 0, kk == C - 1)
            last.then_inc(sig.g1_done, 1)
            project("K0", hh)
            pe.wait_ge(sig.g_lo_ready, 2)
            pe.wait_ge(sig.gt_lo_ready, 1)
            pe.wait_ge(sig.norm_ready, 2)
            pe.wait_ge(sig.tok_ready, 1)
            for h in range(HEADS):
                hs = slice(h * DK, (h + 1) * DK)
                three_products(ps[:, 4 + h, :], (g2_hi[:, hs], g2_lo[:, hs]), (gt_hi[:], gt_lo[:]), True, True)\
                    .then_inc(sig.z_done, 1)
            project_rows("V0", hh, T)
            project("R0", hh)
            gla_scores(0)
            gla_updates(0)
            project_rows("V1", hh, T)
            gla_outputs(0)
            gla_scores(1)
            gla_updates(1)
            project("R1", hh)
            gla_norm(0)
            gla_outputs(1)
            project("Q1", hh)
            gla_norm(1)
            project("K1", hh)
            project_rows("V2", hh, T)
            gla_scores(2)
            gla_updates(2)
            for pair in range(4):
                if pair == 0:
                    pe.wait_ge(sig.o_lo_ready, 2)
                project(("OUT", 0, pair), oo, nrows=4)
            project("R2", hh)
            gla_outputs(2)
            project_rows("V3", hh, T)
            gla_norm(2)
            gla_scores(3)
            gla_updates(3)
            project("R3", hh)
            gla_outputs(3)
            transpose_memory(0)
            cross_keys(0, (0,))
            gla_norm(3)
            cross_keys(0, (1, 2, 3))
            for pair in range(4):
                if pair == 0:
                    pe.wait_ge(sig.o_lo_ready, 4)
                project(("OUT", 1, pair), oo, nrows=4)
            cross(0)
            ffn(1)
            ffn(2, between=lambda: transpose_memory(1))
            cross_keys(1, (0,))
            norm(5)
            cross_keys(1, (1, 2, 3))
            w = at["pool"].slot
            pe.wait_ge(sig.w_lo_ready, w + 1)
            for g in range(4):
                pe.wait_ge(sig.p_lo_ready, g + 1)
                for c in range(2):
                    bank = chunk_bank(at["pool"].out + 2 * g + c)
                    for kk in range(2):
                        last = three_products(ps[:, bank, :], weights(w % 2, 2 * g + kk, c),
                                              (p_hi[:, 2 * (g % 2) + kk, :], p_lo[:, 2 * (g % 2) + kk, :]),
                                              kk == 0, kk == 1)
                    last.then_inc(sig.part_done, 1)
            cross(1)
            ffn(3)
            for piece in range(2 * T):
                tile, half = piece % T, piece // T
                if piece == 0:
                    pe.wait_ge(sig.evacuated, OUTS)
                if piece == T:
                    norm(LAST)
                if piece == 2 * T - 1:
                    pe.wait_ge(sig.y_out_by_dve, 1)
                for c in range(4):
                    m = 4 * half + c
                    if tile == 0:
                        pe.wait_ge(sig.y_ready, m + 1)
                    last = nc.tensor.transpose(ps[:, OUT_BANK[piece], c * P:(c + 1) * P],
                                               x[:, m, tile * P:(tile + 1) * P], ident[:])
                last.then_inc(sig.y_transposed, 1)

        @block.scalar
        def _(act):
            def hi_part(out_ap, in_ap, **kw):
                return nc.scalar.activation(out_ap, in_ap, ACT.Copy, **kw)

            def split_hi(s, loaded, done, nrows):
                act.wait_ge(raw_loaded[s], loaded)
                if done is not None:
                    act.wait_ge(sig.part_done, done)
                hi_part(w_hi[:, s, 0:nrows, :], raw[:, s, 0:nrows, :]).then_inc(sig.w_hi_ready, 1)

            def split_next(w):
                if w + 2 < SLOTS:
                    split_hi(w % 2, 16 * ((w + 2) // 2 + 1), slot_end[w], slot_rows[w + 2])

            def feed(f, m):
                act.wait_ge(*x_final(f, m))
                if f in H_BASE:
                    hi_part(h_hi[:, m, :], x[:, m, :], scale=gain(f, m)).then_inc(sig.h_hi_ready, 1)
                if C * f + m >= 2:
                    act.wait_ge(sig.sq_added, C * f + m - 1)
                nc.scalar.activation(sq[:, m % 2, :], x[:, m, :], ACT.Square).then_inc(sig.sq_ready, 1)

            def norm_roots(f):
                act.wait_ge(sig.norm_summed, f + 1)
                if f in RMS_FEEDS:
                    nc.scalar.activation(rms[:], ps[:, 4, :], ACT.Sqrt, bias=eps[:], scale=1.0 / D)\
                      .then_inc(sig.norm_root, 1)
                if f in TOK_FEEDS:
                    nc.scalar.activation(rms_tok[:], ps[:, 5, 0:T], ACT.Sqrt, bias=eps[:], scale=1.0 / D)\
                      .then_inc(sig.tok_root, 1)

            def ffn(n):
                norm_roots((0, 3, 4, 7)[n])
                w0, p0, o0 = at[("gu", n, 0)].slot, at[("gu", n, 0)].part, at[("gu", n, 0)].out
                with act.Fori(0, FC // 2) as j:
                    for c in range(2):
                        act.wait_ge(sig.evacuated, o0 + c + 1 + 4 * j)
                        nc.scalar.activation(t[:, c, :], t[:, c, :], ACT.Silu).then_inc(sig.silu_done, 1)
                    split_hi(w0 % 2, j * 16 + 16 * ((w0 + 2) // 2 + 1), p0 + 2 + 4 * j, C)
                    for c in range(2):
                        act.wait_ge(sig.evacuated, o0 + c + 3 + 4 * j)
                        hi_part(mid_hi[:, 2 * j + c, :], t[:, c, :]).then_inc(sig.mid_hi_ready, 1)
                    split_hi((w0 + 1) % 2, j * 16 + 16 * ((w0 + 3) // 2 + 1), p0 + 4 + 4 * j, C)
                for pair in range(C // 2):
                    for g in range(len(GROUPS)):
                        if g == len(GROUPS) - 1:
                            for m in (2 * pair, 2 * pair + 1):
                                feed(FEED_AFTER[n], m)
                        split_next(at[("down", n, pair, g)].slot)

            def part(name, c):
                act.wait_ge(sig.part_done, at[name].part + c + 1)
                return (at[name].out + c) % 4

            def gates(pair):
                act.wait_ge(sig.gate_neg, pair + 1)
                nc.scalar.activation(u[:], u[:], ACT.Exp).then_inc(sig.gate_exp, 1)
                act.wait_ge(sig.gate_exp, pair + 1)
                nc.scalar.activation(u[:], u[:], ACT.Ln, bias=1.0).then_inc(sig.gate_ln, 1)

            def decayed_qk(h):
                act.wait_ge(sig.diff_ready, h + 1)
                nc.scalar.activation(e[:, 1, :], e[:, 0, :], ACT.Exp, scale=-1.0 / TAU).then_inc(sig.exp_ready, 1)
                nc.scalar.activation(e[:, 0, :], e[:, 0, :], ACT.Exp, scale=1.0 / TAU).then_inc(sig.exp_ready, 1)
                act.wait_ge(sig.qk_scaled, 2 * h + 2)
                if h > 0:
                    act.wait_ge(sig.a_done, h)
                hi_part(qk_hi[:], e[:]).then_inc(sig.qk_hi_ready, 1)
                act.wait_ge(sig.last_diff, h + 1)
                nc.scalar.activation(e[:, 0, :], e[:, 0, :], ACT.Exp, scale=1.0 / TAU).then_inc(sig.last_exp, 1)

            def scores_split(h):
                act.wait_ge(sig.a_done, h + 1)
                hi_part(kst_hi[:], ps[:, 4, :].rearrange("p (t d) -> p t d", t=T)).then_inc(sig.kst_hi_ready, 1)
                act.wait_ge(sig.at_ready, h + 1)
                hi_part(am_hi[:], acc[:].rearrange("p (t d) -> p t d", t=T)).then_inc(sig.at_hi_ready, 1)

            def entering_q(h):
                nc.scalar.activation(e[:, 1, :], b[:, h, :], ACT.Exp, scale=1.0 / TAU).then_inc(sig.in_exp, 1)
                if h > 0:
                    act.wait_ge(sig.s_ready, 7 * h)
                nc.scalar.activation(decay[:], b[:, h, :].rearrange("p (n c) -> p n c", c=CH)[:, :, CH - 1], ACT.Exp,
                                     scale=1.0 / TAU).then_inc(sig.decay_ready, 1)
                act.wait_ge(sig.qin_ready, h + 1)
                hi_part(qin_hi[:], e[:, 1, :]).then_inc(sig.qin_hi_ready, 1)

            def states(h):
                for n in range(NCH - 1):
                    act.wait_ge(sig.s_ready, 7 * h + n + 1)
                    hi_part(S_hi[:, n, :], S[:, n % 2, :]).then_inc(sig.s_hi_ready, 1)

            def values(h):
                for tt in range(T):
                    bank = part(f"V{h}", tt)
                    hi_part(v_hi[:, h % 2, tt, :], ps[:, bank, 0:DV], scale=rms_tok[:, tt:tt + 1])\
                        .then_inc(sig.v_hi_ready, 1)
                split_next(at[f"V{h}"].slot)

            def output_gate(h):
                for c in range(2):
                    act.wait_ge(sig.evacuated, at[f"R{h}"].out + c + 1)
                    nc.scalar.activation(t[:, c, :], t[:, c, :], ACT.Silu).then_inc(sig.r_silu, 1)
                split_next(at[f"R{h}"].slot)

            def outputs(h):
                for c in range(2):
                    bank = part(f"c{h}", c)
                    nc.scalar.activation(sq[:, c, :], ps[:, bank, :], ACT.Square).then_inc(sig.o_squared, 1)

            def value_norm(h):
                act.wait_ge(sig.o_summed, h + 1)
                nc.scalar.activation(sq[:, 0, :], ps[:, 4, :], ACT.Sqrt, bias=eps[:], scale=1.0 / DV)\
                  .then_inc(sig.o_root, 1)
                act.wait_ge(sig.o_scaled, 2 * h + 2)
                hi_part(o_hi[:, 2 * (h % 2):2 * (h % 2) + 2, :], u[:]).then_inc(sig.o_hi_ready, 1)

            def memory_scale(i):
                act.wait_ge(sig.mem_loaded, 16 * (i + 1))
                junk = (e, t)[i]
                for mt in range(MT):
                    if mt:
                        act.wait_ge(sig.mem_squared, MT * i + mt)
                    nc.scalar.activation(junk[:].rearrange("p a b -> p (a b)"), mem_tok[i][:, mt, :], ACT.Square,
                                         accum_out=mem_rms[:, mt:mt + 1]).then_inc(sig.mem_squared, 1)
                act.wait_ge(sig.mem_squared, MT * (i + 1))
                nc.scalar.activation(mem_rms[:], mem_rms[:], ACT.Sqrt, bias=eps[:], scale=1.0 / D)\
                  .then_inc(sig.mem_root, 1)
                act.wait_ge(sig.mem_rms_ready, i + 1)
                for mt in range(MT):
                    nc.scalar.activation(mem_tok[i][:, mt, :], mem_tok[i][:, mt, :], ACT.Copy,
                                         scale=mem_rms[:, mt:mt + 1]).then_inc(sig.mem_scaled, 1)

            def memory(i):
                for c in range(C):
                    act.wait_ge(sig.mem_transposed, C * i + c // 2 * 2 + 2)
                    hi_part(m_hi[:, c, :], ps[:, 4 + c // 2, (c % 2) * MEM:(c % 2 + 1) * MEM],
                            scale=col("n_mem", i * C + c)).then_inc(sig.m_hi_ready, 1)

            def cross_keys(i, pairs):
                for pair in pairs:
                    for c in range(2):
                        bank = part(("xk", i, pair), c)
                        hi_part(xk_hi[:, 2 * pair + c, :], ps[:, bank, 0:MEM]).then_inc(sig.xk_hi_ready, 1)
                    split_next(at[("xk", i, pair)].slot)

            def pooled(g):
                act.wait_ge(sig.mean_ready, g + 1)
                if g >= 2:
                    act.wait_ge(sig.part_done, at["pool"].part + 2 * (g - 1))
                hi_part(p_hi[:, 2 * (g % 2):2 * (g % 2) + 2, :], sums[:, g % 2, :, PAD:PAD + SEQ])\
                    .then_inc(sig.p_hi_ready, 1)

            def softmax(i, h):
                n = HEADS * i + h
                act.wait_ge(sig.neg_max_ready, n + 1)
                for tt in range(T):
                    nc.scalar.activation(p_tok[:, h, tt, :],
                                         ps[:, 4 + 2 * (h % 2) + tt // 2, (tt % 2) * MEM:(tt % 2 + 1) * MEM],
                                         ACT.Exp, bias=sbias[:, tt:tt + 1], scale=rms_tok[:, tt:tt + 1],
                                         accum_out=ssum[:, tt:tt + 1]).then_inc(sig.exp_done, 1)

            def p_split(i, h):
                n = HEADS * i + h
                act.wait_ge(sig.p_transposed, n + 1)
                if 1 <= h <= 2:
                    act.wait_ge(sig.part_done, at[("pv", i, h - 1)].part + 2)
                hi_part((pT_hi, pT3_hi)[h == 3][:], ps[:, 4 + 2 * (h % 2):6 + 2 * (h % 2), :])\
                    .then_inc(sig.pT_hi_ready, 1)

            def cross_values(i, h):
                for mt in range(MT):
                    bank = part(("xv", i, h), mt)
                    hi_part(xv_hi[:, mt, h * DH:(h + 1) * DH], ps[:, bank, 0:COLS]).then_inc(sig.xv_hi_ready, 1)
                split_next(at[("xv", i, h)].slot)

            def cross_outputs(i, h):
                for c in range(2):
                    bank = part(("pv", i, h), c)
                    hi_part(xo_hi[:, 2 * h + c, :], ps[:, bank, :]).then_inc(sig.xo_hi_ready, 1)

            def cross(i):
                for h in range(4):
                    if h == 1:
                        norm_roots(4 * i + 2)
                    for c in range(2):
                        bank = part(("xq", i, h), c)
                        if h >= 2 and c == 0:
                            act.wait_ge(sig.scores_done, HEADS * i + h - 1)
                        hi_part(xq_hi[:, 2 * (h % 2) + c, :], ps[:, bank, :]).then_inc(sig.xq_hi_ready, 1)
                    split_next(at[("xq", i, h)].slot)
                    if h:
                        softmax(i, h - 1)
                cross_values(i, 0)
                softmax(i, 3)
                p_split(i, 0)
                for h in range(1, 4):
                    cross_values(i, h)
                    if h == 3:
                        p_split(i, h)
                    cross_outputs(i, h - 1)
                    if h < 3:
                        p_split(i, h)
                cross_outputs(i, 3)
                for pair in range(4):
                    for m in (2 * pair, 2 * pair + 1):
                        feed(4 * i + 3, m)
                    split_next(at[("xo", i, pair)].slot)

            act.wait_ge(sig.consts_ready, 4)
            act.wait_ge(sig.cols_ready, 1)
            for m in range(C):
                feed(0, m)
                if m % 4 == 3:
                    split_hi(m // 4, 16, None, C)
            ffn(0)
            norm_roots(1)
            act.wait_ge(sig.gates_loaded, 32)
            hi_part(g1_hi[:], g1[:]).then_inc(sig.g_hi_ready, 1)
            hi_part(g2_hi[:], g2[:]).then_inc(sig.g_hi_ready, 1)
            split_next(at["Q0"].slot)
            act.wait_ge(sig.gt_ready, 1)
            hi_part(gt_hi[:], gt[:]).then_inc(sig.gt_hi_ready, 1)
            split_next(at["K0"].slot)
            gates(0)
            gates(1)
            values(0)
            decayed_qk(0)
            output_gate(0)
            scores_split(0)
            entering_q(0)
            states(0)
            values(1)
            decayed_qk(1)
            outputs(0)
            scores_split(1)
            entering_q(1)
            states(1)
            output_gate(1)
            value_norm(0)
            outputs(1)
            split_next(at["Q1"].slot)
            value_norm(1)
            split_next(at["K1"].slot)
            decayed_qk(2)
            values(2)
            scores_split(2)
            entering_q(2)
            states(2)
            for pair in range(4):
                split_next(at[("OUT", 0, pair)].slot)
            output_gate(2)
            decayed_qk(3)
            outputs(2)
            values(3)
            value_norm(2)
            scores_split(3)
            entering_q(3)
            states(3)
            output_gate(3)
            memory_scale(0)
            outputs(3)
            memory(0)
            cross_keys(0, (0,))
            value_norm(3)
            cross_keys(0, (1, 2, 3))
            for pair in range(4):
                for m in (2 * pair, 2 * pair + 1):
                    feed(2, m)
                split_next(at[("OUT", 1, pair)].slot)
            cross(0)
            ffn(1)
            memory_scale(1)
            ffn(2)
            memory(1)
            cross_keys(1, (0,))
            norm_roots(5)
            cross_keys(1, (1, 2, 3))
            pooled(0)
            pooled(1)
            for g in range(4):
                for m in (2 * g, 2 * g + 1):
                    feed(6, m)
                if g < 2:
                    pooled(g + 2)
            split_next(at["pool"].slot)
            cross(1)
            ffn(3)
            norm_roots(LAST)
            for piece in range(1, 2 * T, 2):
                tile, half = piece % T, piece // T
                act.wait_ge(sig.y_transposed, piece + 1)
                act.wait_ge(sig.tok_ready, len(TOK_FEEDS))
                nc.scalar.activation(y_tok[:, tile, half * 512:(half + 1) * 512], ps[:, OUT_BANK[piece], :], ACT.Copy,
                                     scale=rms_tok[:, tile:tile + 1]).then_inc(sig.y_out_by_act, 1)

        @block.vector
        def _(dve):
            def lo_part(out_ap, value, hi):
                return nc.vector.tensor_tensor(out_ap, value, hi.bitcast(F32), ALU.subtract)

            def scaled_lo_part(out_ap, value, scale, hi):
                return nc.vector.scalar_tensor_tensor(out_ap, value, scale, hi.bitcast(F32), ALU.mult, ALU.subtract)

            def split_lo(s, hi_count, nrows):
                dve.wait_ge(sig.w_hi_ready, hi_count)
                lo_part(w_lo[:, s, 0:nrows, :], raw[:, s, 0:nrows, :], w_hi[:, s, 0:nrows, :])\
                    .then_inc(sig.w_lo_ready, 1)

            def split_next(w):
                if w + 2 < SLOTS:
                    split_lo(w % 2, w + 3, slot_rows[w + 2])

            def part(name, c):
                dve.wait_ge(sig.part_done, at[name].part + c + 1)
                return (at[name].out + c) % 4

            def feed(f, m):
                if f == LAST:
                    dve.wait_ge(sig.sq_ready, C * f + m + 1)
                    dve.wait_ge(*x_final(f, m))
                    nc.vector.tensor_scalar_mul(x[:, m, :], x[:, m, :], gain(f, m)).then_inc(sig.y_ready, 1)
                elif f in H_BASE:
                    dve.wait_ge(sig.h_hi_ready, H_BASE[f] + m + 1)
                    scaled_lo_part(h_lo[:, m, :], x[:, m, :], gain(f, m), h_hi[:, m, :]).then_inc(sig.h_ready, 1)

            def norm_inverses(f):
                if f in RMS_FEEDS:
                    dve.wait_ge(sig.norm_root, RMS_FEEDS.index(f) + 1)
                    nc.vector.reciprocal(rms[:], rms[:]).then_inc(sig.norm_ready, 1)
                if f in TOK_FEEDS:
                    n = TOK_FEEDS.index(f) + 1
                    dve.wait_ge(sig.tok_root, n)
                    if f in (2, 6):
                        nc.vector.reciprocal(rms_tok[:], rms_tok[:]).then_inc(sig.tok_inverse, 1)
                        dve.wait_ge(sig.tok_inverse, f // 6 + 1)
                        nc.vector.tensor_scalar_mul(rms_tok[:], rms_tok[:], float(DH) ** -0.5)\
                          .then_inc(sig.tok_ready, 1)
                    else:
                        nc.vector.reciprocal(rms_tok[:], rms_tok[:]).then_inc(sig.tok_ready, 1)
                if f in RMS_FEEDS:
                    dve.wait_ge(sig.norm_ready, RMS_FEEDS.index(f) + 1)
                if f in TOK_FEEDS:
                    dve.wait_ge(sig.tok_ready, n)

            def ffn(n):
                norm_inverses((0, 3, 4, 7)[n])
                w0, p0 = at[("gu", n, 0)].slot, at[("gu", n, 0)].part
                o0 = at[("gu", n, 0)].out
                with dve.Fori(0, FC // 2) as j:
                    for c in range(2):
                        dve.wait_ge(sig.part_done, p0 + c + 1 + 4 * j)
                        nc.vector.tensor_tensor(t[:, c, :], ps[:, (o0 + c) % 4, :], rms[:], ALU.mult)\
                          .then_inc(sig.evacuated, 1)
                    split_lo(w0 % 2, w0 + 3 + 2 * j, C)
                    for c in range(2):
                        dve.wait_ge(sig.part_done, p0 + c + 3 + 4 * j)
                        dve.wait_ge(sig.silu_done, FC * n + c + 1 + 2 * j)
                        nc.vector.tensor_tensor(t[:, c, :], t[:, c, :], ps[:, (o0 + 2 + c) % 4, :], ALU.mult)\
                          .then_inc(sig.evacuated, 1)
                    for c in range(2):
                        dve.wait_ge(sig.mid_hi_ready, FC * n + c + 1 + 2 * j)
                        lo_part(mid_lo[:, 2 * j + c, :], t[:, c, :], mid_hi[:, 2 * j + c, :]).then_inc(sig.mid_ready, 1)
                    split_lo((w0 + 1) % 2, w0 + 4 + 2 * j, C)
                    dve.wait_ge(sig.mid_ready, FC * n + 2 + 2 * j)
                for pair in range(C // 2):
                    for g in range(len(GROUPS)):
                        name = ("down", n, pair, g)
                        if g == len(GROUPS) - 1:
                            for c in range(2):
                                m, o = 2 * pair + c, at[name].out + c
                                bank = part(name, c)
                                nc.vector.scalar_tensor_tensor(t[:, c, :], ps[:, bank, :], 0.5, rms[:], ALU.mult,
                                                               ALU.mult).then_inc(sig.evacuated, 1)
                                dve.wait_ge(sig.evacuated, o + 1)
                                nc.vector.tensor_tensor(x[:, m, :], x[:, m, :], t[:, c, :], ALU.add)\
                                  .then_inc(sig.x_ready, 1)
                                feed(FEED_AFTER[n], m)
                        split_next(at[name].slot)

            def plain_residual(name, f, m, signal_half=False):
                bank = part(name, m % 2)
                nc.vector.tensor_tensor(x[:, m, :], ps[:, bank, :], x[:, m, :], ALU.add).then_inc(sig.evacuated, 1)
                if f is not None:
                    feed(f, m)

            def gates(pair):
                hs = slice(2 * pair, 2 * pair + 2)
                nc.vector.scalar_tensor_tensor(u[:], b[:, hs, :], -1.0, b[:, hs, :], ALU.mult, ALU.min)\
                  .then_inc(sig.gate_neg, 1)
                dve.wait_ge(sig.gate_ln, pair + 1)
                nc.vector.scalar_tensor_tensor(e[:], b[:, hs, :], 0.0, u[:], ALU.min, ALU.subtract)\
                  .then_inc(sig.gate_log, 1)
                dve.wait_ge(sig.gate_log, pair + 1)
                dve.wait_ge(sig.scanmask_ready, 2)
                for c in range(2):
                    nc.vector.tensor_tensor_scan(b[:, 2 * pair + c, :], acc[:], e[:, c, :], 0.0, ALU.mult, ALU.add)\
                      .then_inc(sig.b_ready, 1)
                dve.wait_ge(sig.b_ready, 2 * pair + 2)

            def by_chunk(ap):
                return ap.rearrange("p (n c) -> p n c", c=CH)

            def decayed_qk(h):
                bc = by_chunk(b[:, h, :])
                if h > 0:
                    dve.wait_ge(sig.qin_lo_ready, h)
                nc.vector.tensor_tensor(by_chunk(e[:, 0, :]), bc, bc[:, :, CH // 2 - 1:CH // 2].broadcast_to([P, NCH, CH]),
                                        ALU.subtract).then_inc(sig.diff_ready, 1)
                dve.wait_ge(sig.exp_ready, 2 * h + 2)
                nc.vector.tensor_tensor(e[:, 0, :], q[:, h % 2, :], e[:, 0, :], ALU.mult).then_inc(sig.qk_scaled, 1)
                nc.vector.tensor_tensor(e[:, 1, :], k[:, h % 2, :], e[:, 1, :], ALU.mult).then_inc(sig.qk_scaled, 1)
                dve.wait_ge(sig.qk_hi_ready, h + 1)
                dve.wait_ge(sig.qk_scaled, 2 * h + 2)
                lo_part(qk_lo[:], e[:], qk_hi[:]).then_inc(sig.qk_lo_ready, 1)
                dve.wait_ge(sig.qk_lo_ready, h + 1)
                nc.vector.tensor_tensor(by_chunk(e[:, 0, :]), bc[:, :, CH - 1:CH].broadcast_to([P, NCH, CH]), bc,
                                        ALU.subtract).then_inc(sig.last_diff, 1)
                dve.wait_ge(sig.last_exp, h + 1)
                nc.vector.tensor_tensor(k[:, h % 2, :], k[:, h % 2, :], e[:, 0, :], ALU.mult).then_inc(sig.kst_ready, 1)

            def scores_split(h):
                dve.wait_ge(sig.kst_hi_ready, h + 1)
                lo_part(kst_lo[:], ps[:, 4, :].rearrange("p (t d) -> p t d", t=T), kst_hi[:]).then_inc(sig.kst_lo_ready, 1)
                masked = acc[:].rearrange("p (t d) -> p t d", t=T)
                if h == 0:
                    nc.vector.memset(acc[:], 0.0).then_inc(sig.at_zeroed, 1)
                    dve.wait_ge(sig.at_zeroed, 1)
                    dve.wait_ge(sig.mask_ready, 2)
                else:
                    dve.wait_ge(sig.at_lo_ready, h)
                nc.vector.copy_predicated(masked, mask[:].bitcast(I32).unsqueeze(1).broadcast_to([P, T, P]),
                                          ps[:, 5, :].rearrange("p (t d) -> p t d", t=T)).then_inc(sig.at_ready, 1)
                dve.wait_ge(sig.at_hi_ready, h + 1)
                lo_part(am_lo[:], masked, am_hi[:]).then_inc(sig.at_lo_ready, 1)

            def entering_q(h):
                dve.wait_ge(sig.in_exp, h + 1)
                nc.vector.tensor_tensor(e[:, 1, :], q[:, h % 2, :], e[:, 1, :], ALU.mult).then_inc(sig.qin_ready, 1)
                dve.wait_ge(sig.qin_hi_ready, h + 1)
                lo_part(qin_lo[:], e[:, 1, :], qin_hi[:]).then_inc(sig.qin_lo_ready, 1)

            def states(h):
                dve.wait_ge(sig.decay_ready, h + 1)
                for n in range(NCH - 1):
                    half, tt = n % 2, n // 2
                    update = ps[:, 4 + 2 * half + tt // 2, (tt % 2) * DV:(tt % 2 + 1) * DV]
                    if n >= 2 or (h > 0 and n == 0):
                        dve.wait_ge(sig.s_lo_ready, 7 * h + max(n - 1, 0))
                    dve.wait_ge(sig.kv_done, 7 * h + UPDATES_BEFORE[n])
                    if n == 0:
                        nc.vector.tensor_copy(S[:, 0, :], update).then_inc(sig.s_ready, 1)
                    else:
                        dve.wait_ge(sig.s_ready, 7 * h + n)
                        nc.vector.scalar_tensor_tensor(S[:, n % 2, :], S[:, (n - 1) % 2, :], decay[:, n:n + 1], update,
                                                       ALU.mult, ALU.add).then_inc(sig.s_ready, 1)
                    dve.wait_ge(sig.s_hi_ready, 7 * h + n + 1)
                    dve.wait_ge(sig.s_ready, 7 * h + n + 1)
                    lo_part(S_lo[:, n, :], S[:, n % 2, :], S_hi[:, n, :]).then_inc(sig.s_lo_ready, 1)

            def values(h):
                for tt in range(T):
                    bank = part(f"V{h}", tt)
                    dve.wait_ge(sig.v_hi_ready, T * h + tt + 1)
                    scaled_lo_part(v_lo[:, h % 2, tt, :], ps[:, bank, 0:DV], rms_tok[:, tt:tt + 1], v_hi[:, h % 2, tt, :])\
                        .then_inc(sig.evacuated, 1)
                split_next(at[f"V{h}"].slot)

            def output_gate(h):
                if h > 0:
                    dve.wait_ge(sig.evacuated, at[f"c{h - 1}"].out + 2)
                for c in range(2):
                    bank = part(f"R{h}", c)
                    nc.vector.tensor_tensor(t[:, c, :], ps[:, bank, :], rms[:], ALU.mult).then_inc(sig.evacuated, 1)
                split_next(at[f"R{h}"].slot)

            def outputs(h):
                if h > 0:
                    dve.wait_ge(sig.o_lo_ready, h)
                for c in range(2):
                    bank = part(f"c{h}", c)
                    dve.wait_ge(sig.o_squared, 2 * h + c + 1)
                    dve.wait_ge(sig.r_silu, 2 * h + c + 1)
                    nc.vector.scalar_tensor_tensor(u[:, c, :], ps[:, bank, :], col("gla_onorm", c), t[:, c, :],
                                                   ALU.mult, ALU.mult).then_inc(sig.evacuated, 1)

            def value_norm(h):
                dve.wait_ge(sig.o_root, h + 1)
                nc.vector.reciprocal(sq[:, 0, :], sq[:, 0, :]).then_inc(sig.o_rms, 1)
                dve.wait_ge(sig.o_rms, h + 1)
                dve.wait_ge(sig.evacuated, at[f"c{h}"].out + 2)
                for c in range(2):
                    nc.vector.tensor_tensor(u[:, c, :], u[:, c, :], sq[:, 0, :], ALU.mult).then_inc(sig.o_scaled, 1)
                dve.wait_ge(sig.o_scaled, 2 * h + 2)
                dve.wait_ge(sig.o_hi_ready, h + 1)
                hs = slice(2 * (h % 2), 2 * (h % 2) + 2)
                lo_part(o_lo[:, hs, :], u[:], o_hi[:, hs, :]).then_inc(sig.o_lo_ready, 1)

            def query_key(name, to, factor):
                for c in range(2):
                    bank = part(name, c)
                    nc.vector.scalar_tensor_tensor(to[:, c, :], ps[:, bank, :], factor, rms[:], ALU.mult, ALU.mult)\
                      .then_inc(sig.evacuated, 1)
                split_next(at[name].slot)
                dve.wait_ge(sig.evacuated, at[name].out + 2)

            def memory_scale(i):
                dve.wait_ge(sig.mem_root, i + 1)
                nc.vector.reciprocal(mem_rms[:], mem_rms[:]).then_inc(sig.mem_rms_ready, 1)

            def memory(i):
                for c in range(C):
                    dve.wait_ge(sig.m_hi_ready, C * i + c // 2 * 2 + 2)
                    scaled_lo_part(m_lo[:, c, :], ps[:, 4 + c // 2, (c % 2) * MEM:(c % 2 + 1) * MEM],
                                   col("n_mem", i * C + c), m_hi[:, c, :]).then_inc(sig.m_lo_ready, 1)

            def evacuate_split(name, c, n, hi_sem, hi_count, lo, hi):
                bank = part(name, c)
                dve.wait_ge(hi_sem, hi_count)
                lo_part(lo, ps[:, bank, 0:n], hi).then_inc(sig.evacuated, 1)

            def cross_keys(i, pairs):
                for pair in pairs:
                    for c in range(2):
                        kk = 2 * pair + c
                        evacuate_split(("xk", i, pair), c, MEM, sig.xk_hi_ready, C * i + kk + 1, xk_lo[:, kk, :],
                                       xk_hi[:, kk, :])
                    split_next(at[("xk", i, pair)].slot)

            def softmax_max(i, h):
                n = HEADS * i + h
                dve.wait_ge(sig.scores_done, n + 1)
                bank = 4 + 2 * (h % 2)
                nc.vector.reduce_max(smax[:], ps[:, bank:bank + 2, :].rearrange("p b (h m) -> p (b h) m", m=MEM),
                                     AX_X).then_inc(sig.max_ready, 1)
                dve.wait_ge(sig.max_ready, n + 1)
                nc.vector.scalar_tensor_tensor(sbias[:], smax[:], -1.0, rms_tok[:], ALU.mult, ALU.mult)\
                  .then_inc(sig.neg_max_ready, 1)

            def softmax_divide(i, h):
                n = HEADS * i + h
                dve.wait_ge(sig.exp_done, T * (n + 1))
                nc.vector.reciprocal(ssum[:], ssum[:]).then_inc(sig.sum_inverted, 1)
                dve.wait_ge(sig.sum_inverted, n + 1)
                for tt in range(T):
                    last = nc.vector.tensor_scalar_mul(p_tok[:, h, tt, :], p_tok[:, h, tt, :], ssum[:, tt:tt + 1])
                last.then_inc(sig.p_ready, 1)

            def p_split(i, h):
                n = HEADS * i + h
                dve.wait_ge(sig.pT_hi_ready, n + 1)
                lo_part((pT_lo, pT3_lo)[h == 3][:], ps[:, 4 + 2 * (h % 2):6 + 2 * (h % 2), :],
                        (pT_hi, pT3_hi)[h == 3][:]).then_inc(sig.pT_lo_ready, 1)

            def cross_values(i, h):
                vs = slice(h * DH, (h + 1) * DH)
                for mt in range(MT):
                    evacuate_split(("xv", i, h), mt, COLS, sig.xv_hi_ready, MT * (HEADS * i + h) + mt + 1,
                                   xv_lo[:, mt, vs], xv_hi[:, mt, vs])
                split_next(at[("xv", i, h)].slot)

            def cross_outputs(i, h):
                for c in range(2):
                    evacuate_split(("pv", i, h), c, SEQ, sig.xo_hi_ready, C * i + 2 * h + c + 1, xo_lo[:, 2 * h + c, :],
                                   xo_hi[:, 2 * h + c, :])

            def cross(i):
                for h in range(4):
                    if h == 1:
                        norm_inverses(4 * i + 2)
                    for c in range(2):
                        at_q = 2 * (h % 2) + c
                        evacuate_split(("xq", i, h), c, SEQ, sig.xq_hi_ready, C * i + 2 * h + c + 1,
                                       xq_lo[:, at_q, :], xq_hi[:, at_q, :])
                    split_next(at[("xq", i, h)].slot)
                    if h:
                        softmax_max(i, h - 1)
                        softmax_divide(i, h - 1)
                cross_values(i, 0)
                softmax_max(i, 3)
                softmax_divide(i, 3)
                p_split(i, 0)
                for h in range(1, 4):
                    cross_values(i, h)
                    if h == 3:
                        p_split(i, h)
                    cross_outputs(i, h - 1)
                    if h < 3:
                        p_split(i, h)
                cross_outputs(i, 3)
                for pair in range(4):
                    for m in (2 * pair, 2 * pair + 1):
                        plain_residual(("xo", i, pair), 4 * i + 3, m)
                    split_next(at[("xo", i, pair)].slot)

            def pooled(g):
                w = WINDOWS[g]
                buf = g % 2
                steps = []
                step = 1
                while step < w:
                    steps.append(step)
                    step *= 2
                src = up[:, 2 * g:2 * g + 2, :]
                for n, step in enumerate(steps):
                    dst = sums[:, (buf + len(steps) - 1 - n) % 2]
                    if g > 0:
                        dve.wait_ge(sig.p_lo_ready, g)
                    nc.vector.tensor_tensor(dst[:, :, PAD:], src[:, :, PAD:], src[:, :, PAD - step:PAD + SEQ - step],
                                            ALU.add).then_inc(sig.window_ready, 1)
                    window_count[0] += 1
                    dve.wait_ge(sig.window_ready, window_count[0])
                    src = dst
                head, body = slice(PAD, 2 * PAD), slice(2 * PAD, PAD + SEQ)
                for c in range(2):
                    nc.vector.tensor_tensor(src[:, c, head], src[:, c, head], inv_count[:, g, :], ALU.mult)\
                      .then_inc(sig.window_ready, 1)
                window_count[0] += 2
                dve.wait_ge(sig.window_ready, window_count[0])
                nc.vector.tensor_tensor(src[:, :, head], src[:, :, head], up[:, 2 * g:2 * g + 2, head], ALU.subtract)\
                  .then_inc(sig.window_ready, 1)
                window_count[0] += 1
                dve.wait_ge(sig.window_ready, window_count[0])
                nc.vector.scalar_tensor_tensor(src[:, :, body], src[:, :, body], 1.0 / w, up[:, 2 * g:2 * g + 2, body],
                                               ALU.mult, ALU.subtract).then_inc(sig.mean_ready, 1)
                dve.wait_ge(sig.p_hi_ready, g + 1)
                dve.wait_ge(sig.mean_ready, g + 1)
                gs = slice(2 * (g % 2), 2 * (g % 2) + 2)
                lo_part(p_lo[:, gs, :], src[:, :, PAD:], p_hi[:, gs, :]).then_inc(sig.p_lo_ready, 1)

            def pool_outputs(g):
                for c in range(2):
                    m, o = 2 * g + c, at["pool"].out + 2 * g + c
                    bank = part("pool", m)
                    nc.vector.tensor_scalar(t[:, c, :], ps[:, bank, :], col("pool_b", m), col("pool_scale", m),
                                            ALU.add, ALU.mult).then_inc(sig.evacuated, 1)
                    dve.wait_ge(sig.evacuated, o + 1)
                    nc.vector.tensor_tensor(x[:, m, :], x[:, m, :], t[:, c, :], ALU.add).then_inc(sig.x_ready, 1)
                    feed(6, m)

            dve.wait_ge(sig.cols_done, 1)
            nc.vector.tensor_copy(cols[:], ps[:, 7, 0:NR]).then_inc(sig.cols_ready, 1)
            dve.wait_ge(sig.cols_ready, 1)
            for m in range(C):
                bank = part(("in", m), 0)
                nc.vector.tensor_copy(x[:, m, :], ps[:, bank, :]).then_inc(sig.evacuated, 1)
                feed(0, m)
                if m % 4 == 3:
                    split_lo(m // 4, m // 4 + 1, C)
            ffn(0)
            norm_inverses(1)
            for n, (lo, value, hi) in enumerate(((g1_lo, g1, g1_hi), (g2_lo, g2, g2_hi))):
                dve.wait_ge(sig.g_hi_ready, n + 1)
                lo_part(lo[:], value[:], hi[:]).then_inc(sig.g_lo_ready, 1)
            query_key("Q0", q, float(DK) ** -0.5)
            dve.wait_ge(sig.g1_done, 1)
            nc.vector.tensor_tensor(gt[:], ps[0:RANK, 6, :], rms[0:RANK, :], ALU.mult).then_inc(sig.gt_ready, 1)
            dve.wait_ge(sig.gt_ready, 1)
            dve.wait_ge(sig.gt_hi_ready, 1)
            lo_part(gt_lo[:], gt[:], gt_hi[:]).then_inc(sig.gt_lo_ready, 1)
            query_key("K0", k, 1.0)
            for h in range(HEADS):
                dve.wait_ge(sig.z_done, h + 1)
                nc.vector.tensor_scalar_add(b[:, h, :], ps[:, 4 + h, :], col("gla_b_g", h)).then_inc(sig.z_biased, 1)
            dve.wait_ge(sig.z_biased, HEADS)
            gates(0)
            gates(1)
            values(0)
            decayed_qk(0)
            output_gate(0)
            scores_split(0)
            entering_q(0)
            states(0)
            values(1)
            decayed_qk(1)
            outputs(0)
            scores_split(1)
            entering_q(1)
            states(1)
            output_gate(1)
            value_norm(0)
            outputs(1)
            query_key("Q1", q, float(DK) ** -0.5)
            value_norm(1)
            query_key("K1", k, 1.0)
            decayed_qk(2)
            values(2)
            scores_split(2)
            entering_q(2)
            states(2)
            for pair in range(4):
                for m in (2 * pair, 2 * pair + 1):
                    plain_residual(("OUT", 0, pair), None, m)
                split_next(at[("OUT", 0, pair)].slot)
            output_gate(2)
            decayed_qk(3)
            outputs(2)
            values(3)
            value_norm(2)
            scores_split(3)
            entering_q(3)
            states(3)
            output_gate(3)
            memory_scale(0)
            outputs(3)
            memory(0)
            cross_keys(0, (0,))
            value_norm(3)
            cross_keys(0, (1, 2, 3))
            for pair in range(4):
                for m in (2 * pair, 2 * pair + 1):
                    plain_residual(("OUT", 1, pair), 2, m)
                split_next(at[("OUT", 1, pair)].slot)
            cross(0)
            ffn(1)
            memory_scale(1)
            ffn(2)
            memory(1)
            nc.vector.memset(inv_count[:, 0, :], 1.0).then_inc(sig.counts_ready, 1)
            dve.wait_ge(sig.counts_ready, 1)
            nc.vector.tensor_tensor_scan(inv_count[:, 3, :], inv_count[:, 0, :], inv_count[:, 0, :], 0.0, ALU.mult,
                                         ALU.add).then_inc(sig.counts_ready, 1)
            dve.wait_ge(sig.counts_ready, 2)
            for g in range(4):
                nc.vector.tensor_scalar_min(inv_count[:, g, :], inv_count[:, 3, :], float(WINDOWS[g]))\
                  .then_inc(sig.counts_ready, 1)
            dve.wait_ge(sig.counts_ready, 6)
            nc.vector.reciprocal(inv_count[:], inv_count[:]).then_inc(sig.counts_ready, 1)
            nc.vector.memset(up[:, :, 0:PAD], 0.0).then_inc(sig.pads_zeroed, 1)
            for buf in range(2):
                nc.vector.memset(sums[:, buf, :, 0:PAD], 0.0).then_inc(sig.pads_zeroed, 1)
            cross_keys(1, (0,))
            norm_inverses(5)
            dve.wait_ge(sig.counts_ready, 7)
            dve.wait_ge(sig.pads_zeroed, 3)
            for m in range(C):
                nc.vector.scalar_tensor_tensor(up[:, m, PAD:], x[:, m, :], gain(5, m), rms[:], ALU.mult, ALU.mult)\
                  .then_inc(sig.up_ready, 1)
            cross_keys(1, (1, 2))
            dve.wait_ge(sig.up_ready, C)
            window_count = [0]
            pooled(0)
            cross_keys(1, (3,))
            pooled(1)
            for g in range(4):
                pool_outputs(g)
                if g < 2:
                    pooled(g + 2)
            split_next(at["pool"].slot)
            cross(1)
            ffn(3)
            norm_inverses(LAST)
            for piece in range(0, 2 * T, 2):
                tile, half = piece % T, piece // T
                dve.wait_ge(sig.y_transposed, piece + 1)
                nc.vector.tensor_scalar_mul(y_tok[:, tile, half * 512:(half + 1) * 512], ps[:, OUT_BANK[piece], :],
                                            rms_tok[:, tile:tile + 1]).then_inc(sig.y_out_by_dve, 1)


def kernel(**inputs):
    import numpy as np
    import concourse.bacc as bacc
    from concourse.bass_utils import run_bass_kernel_spmd

    nc = bacc.Bacc("TRN2", target_bir_lowering=False, num_devices=1)
    arrays, io = {}, {}
    for name, value in inputs.items():
        array = np.ascontiguousarray(value)
        arrays[f"in_{name}"] = array
        io[name] = nc.dram_tensor(f"in_{name}", array.shape, mybir.dt.from_np(array.dtype), kind="ExternalInput").ap()
    shape = arrays["in_x"].shape
    out = nc.dram_tensor("out", shape, F32, kind="ExternalOutput").ap()
    trunk(nc, namedtuple("Inputs", io)(**io), out)
    result = run_bass_kernel_spmd(nc, [arrays], core_ids=[0])
    return result.results[0]["out"]
```

```python
from collections import namedtuple
from contextlib import ExitStack

import concourse.bass as bass
from concourse import mybir

F32 = mybir.dt.float32
F32R = mybir.dt.float32r
I32 = mybir.dt.int32
ALU = mybir.AluOpType
ACT = mybir.ActivationFunctionType
AX_X = mybir.AxisListType.X

P = 128
KB = 1024


def trunk(nc, io, out):
    _, SEQ, D = io.x.shape
    MEM = io.mem.shape[1]
    D_FF = io.ffn1_w_down.shape[1]
    T = SEQ // P
    C = D // P
    FC = D_FF // P
    HEADS = 4
    DK = D // 2 // HEADS
    DV = D // HEADS
    RANK = io.gla_w_g1.shape[2]
    TAU = 16.0
    CH = 64
    NCH = SEQ // CH
    DH = D // HEADS
    MT = MEM // P
    EPS = 1e-6
    WINDOWS = (2, 4, 8, 16)
    PAD = WINDOWS[-1]
    GROUPS = ((0, 8), (8, 8), (16, 6))
    COLS = 256
    assert (SEQ, D, DK, DV, MT, FC) == (512, 1024, P, 2 * P, 2, 22)

    at, slot_end, slot_rows = {}, [], []
    Place = namedtuple("Place", "slot part out")
    placed = {"parts": 0, "outs": 0}

    def place(name, parts, outs, rows=0):
        at[name] = Place(len(slot_end), placed["parts"], placed["outs"])
        placed["parts"] += parts
        placed["outs"] += outs
        if rows:
            slot_end.append(placed["parts"])
            slot_rows.append(rows)

    def place_ffn(n):
        for s in range(FC):
            place(("gu", n, s), 2, 2, C)
        for pair in range(C // 2):
            for g, (_, rows) in enumerate(GROUPS):
                place(("down", n, pair, g), 2, 2 if g == len(GROUPS) - 1 else 0, rows)

    def place_cross_keys(i):
        for pair in range(4):
            place(("xk", i, pair), 2, 2, C)

    CROSS_ORDER = ((("xq", 0), ("xq", 1), ("xq", 2), ("xq", 3), ("xv", 0), ("xv", 1), ("pv", 0), ("xv", 2), ("pv", 1),
                    ("xv", 3), ("pv", 2), ("pv", 3)),
                   (("xq", 0), ("xq", 1), ("xq", 2), ("xq", 3), ("pv", 0), ("pv", 1), ("pv", 2), ("pv", 3)))

    def place_cross(i):
        for kind, h in CROSS_ORDER[i]:
            place((kind, i, h), 2, 2, 0 if kind == "pv" else C)
        for pair in range(4):
            place(("xo", i, pair), 2, 2, C)

    GLA_ORDER = ("Q0", "K0", "V0", "R0", "V1", "R1", "c0", "Q1", "K1", "V2", "c1", "R2", "V3", ("OUT", 0, 0), "c2",
                 ("OUT", 0, 1), ("OUT", 0, 2), ("OUT", 0, 3), "R3", "c3")

    def place_gla():
        for name in GLA_ORDER:
            if name[0] == "c":
                place(name, 2, 2)
            elif name[0] == "OUT":
                place(name, 2, 2, 4)
            else:
                place(name, *((4, 4) if name[0] == "V" else (2, 2)), C)
        place_cross_keys(0)
        for pair in range(4):
            place(("OUT", 1, pair), 2, 2, 4)
        place_cross(0)

    def place_rest():
        place_ffn(1)
        place_ffn(2)
        place_cross_keys(1)
        for h in range(4):
            place(("xv", 1, h), 2, 2, C)
        place("pool", 8, 8, C)
        place_cross(1)
        place_ffn(3)

    for m in range(C):
        place(("in", m), 1, 1)
    place_ffn(0)
    place_gla()
    place_rest()
    SLOTS = len(slot_end)

    OUTS = placed["outs"]

    LAST = 8
    H_BASE = {0: 0, 1: 8, 2: 16, 3: 24, 4: 32, 6: 40, 7: 48}

    ctx = ExitStack()
    with ctx:
        def sb(name, shape, dt=F32):
            return ctx.enter_context(nc.sbuf_tensor(name, shape, dt))

        def sem(name):
            return ctx.enter_context(nc.semaphore(name))

        x = sb("x", [P, C, SEQ])
        h_hi, h_lo = sb("h_hi", [P, C, SEQ], F32R), sb("h_lo", [P, C, SEQ], F32R)
        raw = sb("raw", [P, 2, C, COLS])
        w_hi, w_lo = sb("w_hi", [P, 2, C, COLS], F32R), sb("w_lo", [P, 2, C, COLS], F32R)
        rms = sb("rms", [P, SEQ])
        rms_tok = sb("rms_tok", [P, T])
        acc = sb("acc", [P, SEQ])
        t = sb("t", [P, 2, SEQ])
        sq = sb("sq", [P, 2, SEQ])
        ident, mask = sb("ident", [P, P]), sb("mask", [P, P])
        mean_d, mean_dv = sb("mean_d", [P, P]), sb("mean_dv", [P, 1])
        eps, idle = sb("eps", [P, 1]), sb("idle", [P, 1])
        o_rms = sb("o_rms", [P, T])
        decay = sb("decay", [P, NCH])
        pool_shift = sb("pool_shift", [P, C])
        inv_count = sb("inv_count", [P, 4, PAD])
        smax, sbias, ssum = sb("smax", [P, T]), sb("sbias", [P, T]), sb("ssum", [P, T])
        mem_rms = sb("mem_rms", [P, MT])

        rows, at_row = [], {}
        for name, vec in (("n_ffn1", io.n_ffn1), ("n_mix", io.n_mix), ("n_xattn", io.n_xattn), ("n_mem", io.n_mem),
                          ("n_ffn2", io.n_ffn2), ("n_final", io.n_final), ("pool_scale", io.pool_scale),
                          ("pool_b", io.pool_b), ("gla_b_g", io.gla_b_g), ("gla_onorm", io.gla_onorm)):
            flat = {1: "(r p) -> r p", 2: "l (r p) -> (l r) p", 3: "l g (r p) -> (l g r) p"}[len(vec.shape)]
            at_row[name] = sum(r.shape[0] for r in rows)
            rows.append(vec.rearrange(flat, p=P))
        NR = sum(r.shape[0] for r in rows)
        cols = sb("cols", [P, NR])

        def col(name, c):
            return cols[:, at_row[name] + c:at_row[name] + c + 1]

        def gain(f, c):
            name, layer = (("n_ffn1", 0), ("n_mix", 0), ("n_xattn", 0), ("n_ffn2", 0), ("n_ffn1", 1), ("n_mix", 1),
                           ("n_xattn", 1), ("n_ffn2", 1), ("n_final", 0))[f]
            return col(name, layer * C + c)

        def region(name, offset, shape, dt=F32):
            with ExitStack() as e:
                if offset:
                    e.enter_context(nc.sbuf_tensor(f"below_{name}", [P, offset // 4], F32))
                return e.enter_context(nc.sbuf_tensor(name, shape, dt))

        x_tok = region("x_tok", 0, [P, T, D])
        vec_rows = region("vec_rows", 88 * KB, [P, P])
        first_rows = region("first_rows", 89 * KB, [P, P])
        mid_hi = region("mid_hi", 0, [P, FC, SEQ], F32R)
        mid_lo = region("mid_lo", 44 * KB, [P, FC, SEQ], F32R)
        o_hi, o_lo = region("o_hi", 0, [P, 4, SEQ], F32R), region("o_lo", 8 * KB, [P, 4, SEQ], F32R)
        u = region("u", 16 * KB, [P, 2, SEQ])
        b = region("b", 20 * KB, [P, HEADS, SEQ])
        q, k = region("q", 28 * KB, [P, 2, SEQ]), region("k", 32 * KB, [P, 2, SEQ])
        v_hi, v_lo = region("v_hi", 36 * KB, [P, 2, T, DV], F32R), region("v_lo", 44 * KB, [P, 2, T, DV], F32R)
        S = region("S", 52 * KB, [P, 2, DV])
        S_hi, S_lo = region("S_hi", 54 * KB, [P, 7, DV], F32R), region("S_lo", 61 * KB, [P, 7, DV], F32R)
        g1 = region("g1", 52 * KB, [P, C, RANK])
        g1_hi = region("g1_hi", 52 * KB + 512, [P, C, RANK], F32R)
        g1_lo = region("g1_lo", 53 * KB, [P, C, RANK], F32R)
        g2 = region("g2", 54 * KB, [RANK, HEADS * DK])
        g2_hi = region("g2_hi", 56 * KB, [RANK, HEADS * DK], F32R)
        g2_lo = region("g2_lo", 58 * KB, [RANK, HEADS * DK], F32R)
        gt = region("gt", 60 * KB, [RANK, SEQ])
        gt_hi = region("gt_hi", 62 * KB, [RANK, SEQ], F32R)
        gt_lo = region("gt_lo", 64 * KB, [RANK, SEQ], F32R)
        qk_hi, qk_lo = region("qk_hi", 68 * KB, [P, 2, SEQ], F32R), region("qk_lo", 72 * KB, [P, 2, SEQ], F32R)
        qin_hi, qin_lo = region("qin_hi", 80 * KB, [P, SEQ], F32R), region("qin_lo", 82 * KB, [P, SEQ], F32R)
        kst_hi, kst_lo = region("kst_hi", 76 * KB, [P, T, DK], F32R), region("kst_lo", 78 * KB, [P, T, DK], F32R)
        am_hi, am_lo = region("am_hi", 84 * KB, [P, T, P], F32R), region("am_lo", 86 * KB, [P, T, P], F32R)
        e = region("e", 88 * KB, [P, 2, SEQ])
        gate = (t, region("gate_odd", 92 * KB, [P, 2, SEQ]))
        mem_tok = (region("mem_tok0", 20 * KB, [P, MT, D]), region("mem_tok1", 88 * KB, [P, MT, D]))
        p_tok = region("p_tok", 0, [P, HEADS, T, MEM])
        pT_hi, pT_lo = region("pT_hi", 16 * KB, [P, MT, SEQ], F32R), region("pT_lo", 20 * KB, [P, MT, SEQ], F32R)
        xv_hi, xv_lo = region("xv_hi", 40 * KB, [P, MT, D], F32R), region("xv_lo", 48 * KB, [P, MT, D], F32R)
        m_hi, m_lo = region("m_hi", 28 * KB, [P, C, MEM], F32R), region("m_lo", 72 * KB, [P, C, MEM], F32R)
        mem_norm = ((m_hi, m_lo), (h_hi, h_lo))
        pT_odd_hi = region("pT_odd_hi", 24 * KB, [P, MT, SEQ], F32R)
        pT_odd_lo = region("pT_odd_lo", 36 * KB, [P, MT, SEQ], F32R)
        xk_hi, xk_lo = region("xk_hi", 56 * KB, [P, C, MEM], F32R), region("xk_lo", 64 * KB, [P, C, MEM], F32R)
        xq_hi, xq_lo = region("xq_hi", 80 * KB, [P, 4, SEQ], F32R), region("xq_lo", 88 * KB, [P, 4, SEQ], F32R)
        xo_hi, xo_lo = region("xo_hi", 56 * KB, [P, C, SEQ], F32R), region("xo_lo", 80 * KB, [P, C, SEQ], F32R)

        probs_T = ((pT_hi, pT_lo), (pT_odd_hi, pT_odd_lo))
        up = region("up", 0, [P, C, PAD + SEQ])
        sums = region("sums", 17 * KB, [P, 2, 2, PAD + SEQ])
        sums_last = region("sums_last", 26 * KB, [P, 3, 2, PAD + SEQ])
        means = (sums[:, 0], sums[:, 1], sums_last[:, 0], sums_last[:, 2])
        p_hi, p_lo = region("p_hi", 72 * KB, [P, 6, SEQ], F32R), region("p_lo", 84 * KB, [P, 6, SEQ], F32R)
        y_tok = region("y_tok", 0, [P, T, D])

        ps = ctx.enter_context(nc.psum_tensor("ps", [P, 8, 512], F32))

        names = """first_loaded first_cols_done vec_loaded gates_loaded identity_ready consts_ready mask_ready
                cols_done cols_ready
                w_hi_ready w_lo_ready part_done evacuated x_ready h_hi_ready h_ready sq_ready sq_added
                norm_summed norm_root norm_ready tok_root rms_spread silu_done mid_hi_ready mid_ready
                g_hi_ready g_lo_ready g1_done gt_ready gt_hi_ready gt_lo_ready z_done z_biased gate_neg gate_exp
                gate_ln gate_log b_ready scanmask_ready diff_ready exp_ready qk_scaled qk_hi_ready qk_lo_ready
                last_diff last_exp kst_ready in_exp decay_ready qin_ready qin_hi_ready qin_lo_ready a_done
                kst_hi_ready kst_lo_ready at_zeroed at_ready at_hi_ready at_lo_ready kv_done s_ready s_hi_ready
                s_lo_ready v_hi_ready r_silu o_squared o_summed o_root o_rms o_spread o_scaled o_hi_ready o_lo_ready
                mem_loaded mem_squared mem_root mem_rms_ready mem_scaled mem_transposed m_hi_ready
                m_lo_ready xk_hi_ready xv_hi_ready xq_hi_ready scores_done max_ready neg_max_ready exp_done
                sum_inverted p_ready p_transposed pT_hi_ready pT_lo_ready xo_hi_ready
                pads_zeroed counts_ready shift_ready up_ready window_ready mean_ready 
                up_gained last_up last_window last_mean p_hi_ready p_lo_ready
                y_ready y_transposed y_out_by_dve y_out_by_act stored
                tok_inverse tok_ready"""
        sig = namedtuple("Semaphores", names)(*[sem(name) for name in names.split()])
        raw_loaded = [sem("raw_loaded_even"), sem("raw_loaded_odd")]
        x_loaded = [sem(f"x_loaded{g}") for g in range(4)]

        block = ctx.enter_context(nc.Block())

        FEED_AFTER = (1, 4, 5, 8)
        X_COUNTED = (1, 4, 5, 6, 8)
        X_OUT = {0: ("in", 0), 2: ("OUT", 1, 0), 3: ("xo", 0, 0), 7: ("xo", 1, 0)}

        def x_final(f, m):
            if f in X_OUT:
                return sig.evacuated, at[X_OUT[f]].out + m + 1
            return sig.x_ready, C * X_COUNTED.index(f) + m + 1

        RMS_FEEDS = (0, 1, 3, 4, 5, 7)
        SUM_FEEDS = (0, 3, 4, 7)
        SPREAD_FEEDS = (1, 5)
        TOK_FEEDS = (1, 2, 5, 6, LAST)
        UPDATE_ORDER = (0, 2, 1, 3, 4, 6, 5)
        UPDATES_BEFORE = (2, 4, 4, 4, 6, 7, 7)
        OUT_BANK = (4, 6, 7, 0, 1, 2, 3, 4)

        def three_products(out_ap, left, right, first, last):
            nc.tensor.matmul(out_ap, left[0], right[0], start=first, stop=False)
            nc.tensor.matmul(out_ap, left[0], right[1], start=False, stop=False)
            return nc.tensor.matmul(out_ap, left[1], right[0], start=False, stop=last)

        @block.sync
        def _(sp):
            def load_x(g):
                sp.dma_start(x_tok[:, :, g * COLS:(g + 1) * COLS],
                             io.x[0].rearrange("(t p) d -> p t d", p=P)[:, :, g * COLS:(g + 1) * COLS])\
                  .then_inc(x_loaded[g], 16)

            def load(w, split_before, nrows, src):
                if split_before is not None:
                    sp.wait_ge(sig.w_lo_ready, split_before)
                sp.dma_start(raw[:, w % 2, 0:nrows, :], src).then_inc(raw_loaded[w % 2], 16)

            def columns(weight, first_row, nrows, first_col):
                view = weight.rearrange("(k p) n -> p k n", p=P)
                return view[:, first_row:first_row + nrows, bass.ds(first_col, COLS)]

            def load_fixed(name, weight, first_row, nrows, first_col):
                w = at[name].slot
                load(w, w - 1 if w >= 2 else None, nrows, columns(weight, first_row, nrows, first_col))

            def load_ffn(n):
                layer = n // 2
                gu, down = ((io.ffn1_w_gu, io.ffn1_w_down), (io.ffn2_w_gu, io.ffn2_w_down))[n % 2]
                w0 = at[("gu", n, 0)].slot
                first = 0
                if n == 0:
                    load_fixed(("gu", 0, 0), gu[layer], 0, C, 0)
                    load_x(2)
                    load_x(3)
                    load_fixed(("gu", 0, 1), gu[layer], 0, C, D_FF)
                    first = 1
                with sp.Fori(first, FC // 2) as j:
                    load(w0, w0 - 1 + 2 * j, C, columns(gu[layer], 0, C, j * COLS))
                    load(w0 + 1, w0 + 2 * j, C, columns(gu[layer], 0, C, j * COLS + D_FF))
                w0 = at[("down", n, 0, 0)].slot
                with sp.Fori(0, 2) as i:
                    for pair in range(2):
                        for g, (row, nrows) in enumerate(GROUPS):
                            s = 3 * pair + g
                            load(w0 + s, w0 + s - 1 + 6 * i, nrows,
                                 columns(down[layer], row, nrows, i * (2 * COLS) + pair * COLS))

            def load_cross_keys(i):
                for pair in range(4):
                    load_fixed(("xk", i, pair), io.x_w_kv[i], 0, C, pair * COLS)

            def load_cross_values(i):
                for h in range(4):
                    load_fixed(("xv", i, h), io.x_w_kv[i], 0, C, D + h * COLS)

            def load_cross(i):
                for pair in range(4):
                    load_fixed(("xq", i, pair), io.x_w_q[i], 0, C, pair * COLS)
                if i == 0:
                    load_cross_values(0)
                for pair in range(4):
                    load_fixed(("xo", i, pair), io.x_w_o[i], 0, C, pair * COLS)

            load_x(0)
            load_x(1)
            load_ffn(0)
            for name in GLA_ORDER:
                if name[0] == "OUT":
                    load_fixed(name, io.gla_w_out[0], 0, 4, name[2] * COLS)
                elif name[0] != "c":
                    first = {"Q": 0, "K": D // 2, "V": D, "R": 2 * D}[name[0]]
                    load_fixed(name, io.gla_w_in[0], 0, C, first + int(name[1]) * COLS)
            load_cross_keys(0)
            for pair in range(4):
                load_fixed(("OUT", 1, pair), io.gla_w_out[0], 4, 4, pair * COLS)
            load_cross(0)
            load_ffn(1)
            load_ffn(2)
            load_cross_keys(1)
            load_cross_values(1)
            w = at["pool"].slot
            load(w, w - 1, C, io.pool_w[0].rearrange("g (k p) n -> p (g k) n", p=P))
            load_cross(1)
            load_ffn(3)
            for piece in range(2 * T):
                tile, half = piece % T, piece // T
                sp.wait_ge((sig.y_out_by_dve, sig.y_out_by_act)[piece % 2], piece // 2 + 1)
                sp.dma_start(out[0].rearrange("(t p) d -> p t d", p=P)[:, tile, half * 512:(half + 1) * 512],
                             y_tok[:, tile, half * 512:(half + 1) * 512]).then_inc(sig.stored, 16)
            sp.wait_ge(sig.stored, 2 * T * 16)

        @block.gpsimd
        def _(pool):
            nc.gpsimd.memset(ident[:], 0.0).then_inc(sig.consts_ready, 1)
            nc.gpsimd.memset(mask[:], 1.0).then_inc(sig.consts_ready, 1)
            nc.gpsimd.memset(mean_d[:], 1.0 / D).then_inc(sig.consts_ready, 1)
            nc.gpsimd.memset(mean_dv[:], 1.0 / DV).then_inc(sig.consts_ready, 1)
            nc.gpsimd.memset(eps[:], EPS).then_inc(sig.consts_ready, 1)
            pool.wait_ge(sig.consts_ready, 5)
            nc.gpsimd.affine_select(out=ident[:], in_=ident[:], compare_op=ALU.not_equal, fill=1.0, base=0,
                                    pattern=[[-1, P]], channel_multiplier=1).then_inc(sig.identity_ready, 1)
            nc.gpsimd.affine_select(out=mask[:], in_=mask[:], compare_op=ALU.is_ge, fill=0.0, base=0,
                                    pattern=[[1, P]], channel_multiplier=-1).then_inc(sig.mask_ready, 1)
            pool.wait_ge(sig.mask_ready, 1)
            nc.gpsimd.memset(mask[0:CH, CH:P], 0.0).then_inc(sig.mask_ready, 1)

            pad = slice(PAD, PAD + SEQ)

            def pool_last_groups():
                nc.gpsimd.memset(sums_last[:, :, :, 0:PAD], 0.0).then_inc(sig.last_window, 1)
                pool.wait_ge(sig.last_window, 1)
                pool.wait_ge(sig.norm_ready, RMS_FEEDS.index(5) + 1)
                pool.wait_ge(sig.pads_zeroed, 3)
                pool.wait_ge(sig.counts_ready, 7)
                ups, windows = 0, 1
                for g in (2, 3):
                    for m in (2 * g, 2 * g + 1):
                        ups += 1
                        pool.wait_ge(sig.up_gained, ups)
                        nc.gpsimd.tensor_tensor(up[:, m, pad], up[:, m, pad], rms[:], ALU.mult).then_inc(sig.last_up, 1)
                    pool.wait_ge(sig.last_up, ups)
                    src, step, buf = up[:, 2 * g:2 * g + 2, :], 1, g - 2
                    while step < WINDOWS[g]:
                        dst = sums_last[:, buf]
                        nc.gpsimd.tensor_tensor(dst[:, :, pad], src[:, :, pad], src[:, :, PAD - step:PAD + SEQ - step],
                                                ALU.add).then_inc(sig.last_window, 1)
                        windows += 1
                        pool.wait_ge(sig.last_window, windows)
                        src, step, buf = dst, 2 * step, g - 2 + (buf - g + 3) % 2
                    head, body = slice(PAD, 2 * PAD), slice(2 * PAD, PAD + SEQ)
                    for c in range(2):
                        nc.gpsimd.tensor_tensor(src[:, c, head], src[:, c, head], inv_count[:, g, :], ALU.mult)\
                          .then_inc(sig.last_window, 1)
                    nc.gpsimd.tensor_tensor(src[:, :, body], src[:, :, body],
                                            inv_count[:, g, PAD - 1:PAD].unsqueeze(1).broadcast_to([P, 2, SEQ - PAD]),
                                            ALU.mult).then_inc(sig.last_window, 1)
                    windows += 3
                    pool.wait_ge(sig.last_window, windows)
                    nc.gpsimd.tensor_tensor(src[:, :, pad], src[:, :, pad], up[:, 2 * g:2 * g + 2, pad], ALU.subtract)\
                      .then_inc(sig.last_mean, 1)

            def add_squares(f):
                for m in range(C):
                    pool.wait_ge(sig.sq_ready, C * f + m + 1)
                    if m == 0:
                        if f > 0:
                            pool.wait_ge(sig.norm_summed, f)
                        if f == 2:
                            pool.wait_ge(sig.at_lo_ready, HEADS)
                        nc.gpsimd.tensor_copy(acc[:], sq[:, 0, :]).then_inc(sig.sq_added, 1)
                    else:
                        pool.wait_ge(sig.sq_added, C * f + m)
                        nc.gpsimd.tensor_tensor(acc[:], acc[:], sq[:, m % 2, :], ALU.add).then_inc(sig.sq_added, 1)

            add_squares(0)
            row = 0
            for vec in rows:
                pool.dma_start(vec_rows[row:row + vec.shape[0], :], vec).then_inc(sig.vec_loaded, 16)
                row += vec.shape[0]
            add_squares(1)
            pool.wait_ge(sig.part_done, at["Q0"].part)
            pool.dma_start(g1[:], io.gla_w_g1[0].rearrange("(k p) r -> p k r", p=P)).then_inc(sig.gates_loaded, 16)
            pool.dma_start(g2[:], io.gla_w_g2[0]).then_inc(sig.gates_loaded, 16)
            pool.wait_ge(sig.norm_summed, 2)
            nc.gpsimd.memset(acc[:], 1.0).then_inc(sig.scanmask_ready, 1)
            pool.wait_ge(sig.scanmask_ready, 1)
            nc.gpsimd.memset(acc[:].rearrange("p (n c) -> p n c", c=CH)[:, :, 0:1], 0.0)\
              .then_inc(sig.scanmask_ready, 1)
            pool.wait_ge(sig.qin_ready, HEADS)
            pool.wait_ge(sig.decay_ready, HEADS)
            pool.dma_start(mem_tok[0][:], io.mem[0].rearrange("(t p) d -> p t d", p=P)).then_inc(sig.mem_loaded, 16)
            for f in (2, 3):
                add_squares(f)
            pool.wait_ge(sig.part_done, at[("gu", 1, 0)].part)
            pool.dma_start(mem_tok[1][:], io.mem[0].rearrange("(t p) d -> p t d", p=P)).then_inc(sig.mem_loaded, 16)
            for f in (4, 5):
                add_squares(f)
            pool_last_groups()
            for f in (6, 7, 8):
                add_squares(f)

        @block.tensor
        def _(pe):
            def chunk_bank(o):
                if o >= 4:
                    pe.wait_ge(sig.evacuated, o - 3)
                return o % 4

            def weights(s, kk, c):
                cs = slice(c * P, (c + 1) * P)
                return w_hi[:, s, kk, cs], w_lo[:, s, kk, cs]

            def project(name, right, nrows=C, k0=0, feed=None, n=SEQ, middle=None, new=None):
                w = at[name].slot
                pe.wait_ge(sig.w_lo_ready, w + 1)
                if feed is not None:
                    banks = [chunk_bank(at[name].out + c) for c in range(2)]
                    for kk in range(nrows):
                        pe.wait_ge(sig.h_ready, H_BASE[feed] + kk + 1)
                        for c in range(2):
                            last = three_products(ps[:, banks[c], :], weights(w % 2, kk, c),
                                                  (right[0][:, kk, :], right[1][:, kk, :]), kk == 0, kk == nrows - 1)
                            if kk == nrows - 1:
                                last.then_inc(sig.part_done, 1)
                    norm(feed)
                    return
                for c in range(2):
                    bank = chunk_bank(at[name].out + c)
                    for kk in range(nrows):
                        if new is not None and c == 0:
                            pe.wait_ge(new[0], new[1] + kk + 1)
                        last = three_products(ps[:, bank, 0:n], weights(w % 2, kk, c),
                                              (right[0][:, k0 + kk, 0:n], right[1][:, k0 + kk, 0:n]),
                                              kk == 0, kk == nrows - 1)
                    last.then_inc(sig.part_done, 1)
                    if middle is not None and c == 0:
                        middle()

            def project_rows(name, left, tiles, middle=None):
                w = at[name].slot
                pe.wait_ge(sig.w_lo_ready, w + 1)
                for tt in range(tiles):
                    bank = chunk_bank(at[name].out + tt)
                    ts = slice(tt * P, (tt + 1) * P)
                    for kk in range(C):
                        last = three_products(ps[:, bank, 0:COLS], (left[0][:, kk, ts], left[1][:, kk, ts]),
                                              (w_hi[:, w % 2, kk, :], w_lo[:, w % 2, kk, :]), kk == 0, kk == C - 1)
                    last.then_inc(sig.part_done, 1)
                    if middle is not None and tt == 1:
                        middle()

            def norm(f):
                pe.wait_ge(sig.sq_added, C * (f + 1))
                pe.wait_ge(sig.consts_ready, 5)
                last = None
                if f in SUM_FEEDS:
                    last = nc.tensor.matmul(ps[:, 4, :], mean_d[:], acc[:], start=True, stop=True)
                if f in TOK_FEEDS:
                    for tt in range(T):
                        last = nc.tensor.matmul(ps[:, 5, tt:tt + 1], acc[:, tt * P:(tt + 1) * P], mean_d[:, 0:1],
                                                start=True, stop=True)
                last.then_inc(sig.norm_summed, 1)

            def spread_rms(f):
                pe.wait_ge(sig.tok_ready, TOK_FEEDS.index(f) + 1)
                for tt in range(T):
                    last = nc.tensor.matmul(ps[:, 4, tt * P:(tt + 1) * P], rms_tok[:, tt:tt + 1].broadcast_to([P, P]),
                                            ident[:], start=True, stop=True)
                last.then_inc(sig.rms_spread, 1)

            def transpose_vectors():
                pe.wait_ge(sig.vec_loaded, 16 * len(rows))
                nc.tensor.transpose(ps[:, 7, 0:NR], vec_rows[0:NR, :], ident[0:NR, 0:NR]).then_inc(sig.cols_done, 1)

            def ffn(n, between=None):
                hh = (h_hi, h_lo)
                for s in range(2):
                    project(("gu", n, s), hh, feed=(0, 3, 4, 7)[n] if s == 0 else None)
                w0, o0 = at[("gu", n, 0)].slot, at[("gu", n, 0)].out
                with pe.Fori(1, FC // 2) as j:
                    for s in range(2):
                        pe.wait_ge(sig.w_lo_ready, w0 + s + 1 + 2 * j)
                        for c in range(2):
                            o = o0 + 2 * s + c
                            pe.wait_ge(sig.evacuated, o - 3 + 4 * j)
                            for kk in range(C):
                                last = three_products(ps[:, o % 4, :], weights((w0 + s) % 2, kk, c),
                                                      (h_hi[:, kk, :], h_lo[:, kk, :]), kk == 0, kk == C - 1)
                            last.then_inc(sig.part_done, 1)
                if between is not None:
                    between()
                w0, o0 = at[("down", n, 0, 0)].slot, at[("down", n, 0, 0)].out
                with pe.Fori(0, 2) as i:
                    for pair in range(2):
                        for g, (k0, nrows) in enumerate(GROUPS):
                            s = 3 * pair + g
                            pe.wait_ge(sig.w_lo_ready, w0 + s + 1 + 6 * i)
                            pe.wait_ge(sig.mid_ready, FC * n + k0 + nrows)
                            for c in range(2):
                                o = o0 + 2 * pair + c
                                if g == 0:
                                    pe.wait_ge(sig.evacuated, o - 3 + 4 * i)
                                for kk in range(nrows):
                                    last = three_products(ps[:, o % 4, :], weights((w0 + s) % 2, kk, c),
                                                          (mid_hi[:, k0 + kk, :], mid_lo[:, k0 + kk, :]),
                                                          k0 + kk == 0, k0 + kk == FC - 1)
                                last.then_inc(sig.part_done, 1)

            pe.wait_ge(sig.identity_ready, 1)
            for m in range(C):
                if m == 1:
                    pe.wait_ge(sig.first_loaded, 16)
                    nc.tensor.transpose(ps[:, 7, 0:2 * C], first_rows[0:2 * C, :], ident[0:2 * C, 0:2 * C])\
                      .then_inc(sig.first_cols_done, 1)
                if m % 2 == 0:
                    pe.wait_ge(x_loaded[m // 2], 16)
                bank = chunk_bank(m)
                for tt in range(T):
                    last = nc.tensor.transpose(ps[:, bank, tt * P:(tt + 1) * P], x_tok[:, tt, m * P:(m + 1) * P],
                                               ident[:])
                last.then_inc(sig.part_done, 1)

            def gla_scores(h):
                pe.wait_ge(sig.kst_ready, h + 1)
                if h == 0:
                    pe.wait_ge(sig.z_biased, HEADS)
                else:
                    pe.wait_ge(sig.s_ready, 7 * h)
                for tt in range(T):
                    ts = slice(tt * P, (tt + 1) * P)
                    nc.tensor.transpose(ps[:, 4, ts], k[:, h % 2, ts], ident[:])
                pe.wait_ge(sig.qk_lo_ready, h + 1)
                for tt in range(T):
                    ts = slice(tt * P, (tt + 1) * P)
                    last = three_products(ps[:, 5, ts], (qk_hi[:, 1, ts], qk_lo[:, 1, ts]),
                                          (qk_hi[:, 0, ts], qk_lo[:, 0, ts]), True, True)
                last.then_inc(sig.a_done, 1)

            def gla_updates(h):
                pe.wait_ge(sig.kst_lo_ready, h + 1)
                pe.wait_ge(sig.at_ready, h + 1)
                pe.wait_ge(sig.evacuated, at[f"V{h}"].out + T)
                for n in UPDATE_ORDER:
                    if n == UPDATE_ORDER[-1] and h > 0:
                        pe.wait_ge(sig.o_scaled, 2 * h)
                    tt, half = n // 2, n % 2
                    rs = slice(half * CH, (half + 1) * CH)
                    bank, cs = 4 + 2 * half + tt // 2, slice((tt % 2) * DV, (tt % 2 + 1) * DV)
                    three_products(ps[:, bank, cs], (kst_hi[rs, tt, :], kst_lo[rs, tt, :]),
                                   (v_hi[rs, h % 2, tt, :], v_lo[rs, h % 2, tt, :]), True, True)\
                        .then_inc(sig.kv_done, 1)

            def gla_outputs(h):
                pe.wait_ge(sig.at_lo_ready, h + 1)
                pe.wait_ge(sig.qin_lo_ready, h + 1)
                for c in range(2):
                    bank = chunk_bank(at[f"c{h}"].out + c)
                    vs = slice(c * P, (c + 1) * P)
                    for tt in range(T):
                        ts = slice(tt * P, (tt + 1) * P)
                        last = three_products(ps[:, bank, ts], (v_hi[:, h % 2, tt, vs], v_lo[:, h % 2, tt, vs]),
                                              (am_hi[:, tt, :], am_lo[:, tt, :]), True, False)
                        for n in (2 * tt, 2 * tt + 1):
                            if n == 0:
                                continue
                            pe.wait_ge(sig.s_lo_ready, 7 * h + n)
                            ns = slice(n * CH, (n + 1) * CH)
                            last = three_products(ps[:, bank, ns], (S_hi[:, n - 1, vs], S_lo[:, n - 1, vs]),
                                                  (qin_hi[:, ns], qin_lo[:, ns]), False, n % 2 == 1)
                    last.then_inc(sig.part_done, 1)

            def gla_norm(h):
                pe.wait_ge(sig.o_squared, 2 * h + 2)
                if h < HEADS - 1:
                    pe.wait_ge(sig.s_ready, 7 * (h + 1))
                else:
                    pe.wait_ge(sig.m_lo_ready, C)
                for tt in range(T):
                    for c in range(2):
                        last = nc.tensor.matmul(ps[:, 7, tt:tt + 1], sq[:, c, tt * P:(tt + 1) * P], mean_dv[:],
                                                start=c == 0, stop=c == 1)
                last.then_inc(sig.o_summed, 1)

            def spread_norm(h):
                pe.wait_ge(sig.o_rms, h + 1)
                for tt in range(T):
                    last = nc.tensor.matmul(ps[:, 7, tt * P:(tt + 1) * P], o_rms[:, tt:tt + 1].broadcast_to([P, P]),
                                            ident[:], start=True, stop=True)
                last.then_inc(sig.o_spread, 1)

            def transpose_memory(i):
                pe.wait_ge(sig.mem_scaled, MT * (i + 1))
                if i == 0:
                    pe.wait_ge(sig.s_ready, 7 * HEADS)
                else:
                    pe.wait_ge(sig.norm_ready, RMS_FEEDS.index(4) + 1)
                for c in range(C):
                    for mt in range(MT):
                        cs = slice((c % 2) * MEM + mt * P, (c % 2) * MEM + (mt + 1) * P)
                        last = nc.tensor.transpose(ps[:, 4 + c // 2, cs], mem_tok[i][:, mt, c * P:(c + 1) * P],
                                                   ident[:])
                    last.then_inc(sig.mem_transposed, 1)

            def cross_keys(i, pairs):
                for pair in pairs:
                    project(("xk", i, pair), mem_norm[i], n=MEM, new=(sig.m_lo_ready, C * i) if pair == 0 else None)

            def scores(i, h):
                n = HEADS * i + h
                pe.wait_ge(sig.evacuated, at[("xq", i, h)].out + 2)
                if i == 0 and h >= 2:
                    pe.wait_ge(sig.exp_done, T * (n - 1))
                elif h >= 2:
                    pe.wait_ge(sig.pT_lo_ready, n - 1)
                else:
                    pe.wait_ge(sig.tok_ready, TOK_FEEDS.index(4 * i + 2) + 1)
                    pe.wait_ge(sig.m_lo_ready, C * (i + 1))
                for tt in range(T):
                    ts = slice(tt * P, (tt + 1) * P)
                    out_ap = ps[:, 4 + 2 * (h % 2) + tt // 2, (tt % 2) * MEM:(tt % 2 + 1) * MEM]
                    for d in range(2):
                        last = three_products(out_ap, (xq_hi[:, 2 * (h % 2) + d, ts], xq_lo[:, 2 * (h % 2) + d, ts]),
                                              (xk_hi[:, 2 * h + d, :], xk_lo[:, 2 * h + d, :]), d == 0, d == 1)
                last.then_inc(sig.scores_done, 1)

            def transpose_p(i, h):
                n = HEADS * i + h
                pe.wait_ge(sig.p_ready, n + 1)
                if i == 0 and h >= 2:
                    pe.wait_ge(sig.pT_lo_ready, n - 1)
                elif i == 0:
                    pe.wait_ge(sig.exp_done, T * (HEADS * i + 3 + h))
                for mt in range(MT):
                    for tt in range(T):
                        last = nc.tensor.transpose(ps[:, 4 + 2 * (h % 2) + mt, tt * P:(tt + 1) * P],
                                                   p_tok[:, h, tt, mt * P:(mt + 1) * P], ident[:])
                last.then_inc(sig.p_transposed, 1)

            def weighted_values(i, h):
                n = HEADS * i + h
                pe.wait_ge(sig.pT_lo_ready, n + 1)
                right = probs_T[h % 2]
                pe.wait_ge(sig.evacuated, at[("xv", i, h)].out + 2)
                for c in range(2):
                    bank = chunk_bank(at[("pv", i, h)].out + c)
                    vs = slice(h * DH + c * P, h * DH + (c + 1) * P)
                    for mt in range(MT):
                        last = three_products(ps[:, bank, :], (xv_hi[:, mt, vs], xv_lo[:, mt, vs]),
                                              (right[0][:, mt, :], right[1][:, mt, :]), mt == 0, mt == MT - 1)
                    last.then_inc(sig.part_done, 1)

            def cross(i):
                hh = (h_hi, h_lo)
                project(("xq", i, 0), hh, feed=4 * i + 2)
                project(("xq", i, 1), hh, middle=lambda: scores(i, 0))
                project(("xq", i, 2), hh, middle=lambda: scores(i, 1))
                if i == 0:
                    project(("xq", 0, 3), hh, middle=lambda: scores(0, 2))
                    project_rows(("xv", 0, 0), mem_norm[0], MT)
                    scores(0, 3)
                    transpose_p(0, 0)
                    project_rows(("xv", 0, 1), mem_norm[0], MT)
                    transpose_p(0, 1)
                    weighted_values(0, 0)
                    transpose_p(0, 2)
                    project_rows(("xv", 0, 2), mem_norm[0], MT)
                    transpose_p(0, 3)
                    weighted_values(0, 1)
                    project_rows(("xv", 0, 3), mem_norm[0], MT)
                    weighted_values(0, 2)
                    weighted_values(0, 3)
                else:
                    def third_scores():
                        scores(1, 2)
                        transpose_p(1, 1)

                    transpose_p(1, 0)
                    project(("xq", 1, 3), hh, middle=third_scores)
                    weighted_values(1, 0)
                    transpose_p(1, 2)
                    scores(1, 3)
                    weighted_values(1, 1)
                    transpose_p(1, 3)
                    weighted_values(1, 2)
                    weighted_values(1, 3)
                for pair in range(4):
                    project_cross_out(i, pair)

            def project_cross_out(i, pair):
                name = ("xo", i, pair)
                w = at[name].slot
                pe.wait_ge(sig.w_lo_ready, w + 1)
                for c in range(2):
                    bank = chunk_bank(at[name].out + c)
                    for kk in range(C):
                        if pair == 0 and c == 0 and kk % 2 == 0:
                            pe.wait_ge(sig.evacuated, at[("pv", i, kk // 2)].out + 2)
                        last = three_products(ps[:, bank, :], weights(w % 2, kk, c), (xo_hi[:, kk, :], xo_lo[:, kk, :]),
                                              kk == 0, kk == C - 1)
                    last.then_inc(sig.part_done, 1)

            ffn(0, between=transpose_vectors)
            hh, oo = (h_hi, h_lo), (o_hi, o_lo)
            project("Q0", hh, feed=1)
            pe.wait_ge(sig.g_lo_ready, 1)
            for kk in range(C):
                last = three_products(ps[0:RANK, 6, :], (g1_hi[:, kk, :], g1_lo[:, kk, :]),
                                      (h_hi[:, kk, :], h_lo[:, kk, :]), kk == 0, kk == C - 1)
            last.then_inc(sig.g1_done, 1)
            spread_rms(1)
            project("K0", hh)
            pe.wait_ge(sig.g_lo_ready, 2)
            pe.wait_ge(sig.gt_lo_ready, 1)
            pe.wait_ge(sig.norm_ready, 2)
            pe.wait_ge(sig.tok_ready, 1)
            for h in range(HEADS):
                hs = slice(h * DK, (h + 1) * DK)
                three_products(ps[:, 4 + h, :], (g2_hi[:, hs], g2_lo[:, hs]), (gt_hi[:], gt_lo[:]), True, True)\
                    .then_inc(sig.z_done, 1)
            project_rows("V0", hh, T)
            project("R0", hh)
            gla_scores(0)
            project_rows("V1", hh, T, middle=lambda: gla_updates(0))
            project("R1", hh)
            gla_outputs(0)
            gla_scores(1)
            project("Q1", hh, middle=lambda: gla_norm(0))
            spread_norm(0)
            project("K1", hh, middle=lambda: gla_updates(1))
            project_rows("V2", hh, T)
            gla_outputs(1)
            gla_scores(2)
            project("R2", hh, middle=lambda: gla_norm(1))
            spread_norm(1)
            project_rows("V3", hh, T, middle=lambda: gla_updates(2))
            pe.wait_ge(sig.o_lo_ready, 2)
            project(("OUT", 0, 0), oo, nrows=4)
            gla_outputs(2)
            project(("OUT", 0, 1), oo, nrows=4)
            gla_scores(3)
            gla_norm(2)
            project(("OUT", 0, 2), oo, nrows=4)
            spread_norm(2)
            gla_updates(3)
            project(("OUT", 0, 3), oo, nrows=4)
            project("R3", hh)
            transpose_memory(0)
            gla_outputs(3)
            cross_keys(0, (0,))
            gla_norm(3)
            cross_keys(0, (1, 2))
            spread_norm(3)
            cross_keys(0, (3,))
            pe.wait_ge(sig.o_lo_ready, 4)
            for pair in range(4):
                project(("OUT", 1, pair), oo, nrows=4)
            cross(0)
            ffn(1)
            ffn(2, between=lambda: transpose_memory(1))
            cross_keys(1, (0,))
            norm(5)
            cross_keys(1, (1,))
            spread_rms(5)
            cross_keys(1, (2, 3))
            for h in range(4):
                project_rows(("xv", 1, h), mem_norm[1], MT)
            w = at["pool"].slot
            pe.wait_ge(sig.w_lo_ready, w + 1)
            for g in range(4):
                pe.wait_ge(sig.p_lo_ready, g + 1)
                for c in range(2):
                    bank = chunk_bank(at["pool"].out + 2 * g + c)
                    for kk in range(2):
                        last = three_products(ps[:, bank, :], weights(w % 2, 2 * g + kk, c),
                                              (p_hi[:, 2 * (g % 3) + kk, :], p_lo[:, 2 * (g % 3) + kk, :]),
                                              kk == 0, kk == 1)
                    last.then_inc(sig.part_done, 1)
            cross(1)
            ffn(3)
            for piece in range(2 * T):
                tile, half = piece % T, piece // T
                if piece == 0:
                    pe.wait_ge(sig.evacuated, OUTS)
                if piece == T:
                    norm(LAST)
                if piece == 2 * T - 1:
                    pe.wait_ge(sig.y_out_by_dve, 1)
                for c in range(4):
                    m = 4 * half + c
                    if tile == 0:
                        pe.wait_ge(sig.y_ready, m + 1)
                    last = nc.tensor.transpose(ps[:, OUT_BANK[piece], c * P:(c + 1) * P],
                                               x[:, m, tile * P:(tile + 1) * P], ident[:])
                last.then_inc(sig.y_transposed, 1)

        @block.scalar
        def _(act):
            def hi_part(out_ap, in_ap, **kw):
                return nc.scalar.activation(out_ap, in_ap, ACT.Copy, **kw)

            def split_hi(s, loaded, done, nrows):
                act.wait_ge(raw_loaded[s], loaded)
                if done is not None:
                    act.wait_ge(sig.part_done, done)
                hi_part(w_hi[:, s, 0:nrows, :], raw[:, s, 0:nrows, :]).then_inc(sig.w_hi_ready, 1)

            def split_next(w):
                if w + 2 < SLOTS:
                    split_hi(w % 2, 16 * ((w + 2) // 2 + 1), slot_end[w], slot_rows[w + 2])

            def feed(f, m):
                act.wait_ge(*x_final(f, m))
                if f in H_BASE:
                    hi_part(h_hi[:, m, :], x[:, m, :], scale=gain(f, m)).then_inc(sig.h_hi_ready, 1)
                if C * f + m >= 2:
                    act.wait_ge(sig.sq_added, C * f + m - 1)
                nc.scalar.activation(sq[:, m % 2, :], x[:, m, :], ACT.Square).then_inc(sig.sq_ready, 1)

            def norm_roots(f):
                act.wait_ge(sig.norm_summed, f + 1)
                if f in SUM_FEEDS:
                    nc.scalar.activation(rms[:], ps[:, 4, :], ACT.Sqrt, bias=eps[:]).then_inc(sig.norm_root, 1)
                if f in TOK_FEEDS:
                    nc.scalar.activation(rms_tok[:], ps[:, 5, 0:T], ACT.Sqrt, bias=eps[:]).then_inc(sig.tok_root, 1)

            def load_silu():
                nc.scalar.activation(idle[:], eps[:], ACT.Silu)

            def ffn(n, between=None):
                norm_roots((0, 3, 4, 7)[n])
                load_silu()
                w0, p0, o0 = at[("gu", n, 0)].slot, at[("gu", n, 0)].part, at[("gu", n, 0)].out
                with act.Fori(0, FC // 2) as j:
                    for c in range(2):
                        act.wait_ge(sig.evacuated, o0 + c + 1 + 4 * j)
                        nc.scalar.activation(t[:, c, :], t[:, c, :], ACT.Silu).then_inc(sig.silu_done, 1)
                    split_hi(w0 % 2, j * 16 + 16 * ((w0 + 2) // 2 + 1), p0 + 2 + 4 * j, C)
                    for c in range(2):
                        act.wait_ge(sig.evacuated, o0 + c + 3 + 4 * j)
                        hi_part(mid_hi[:, 2 * j + c, :], t[:, c, :]).then_inc(sig.mid_hi_ready, 1)
                    split_hi((w0 + 1) % 2, j * 16 + 16 * ((w0 + 3) // 2 + 1), p0 + 4 + 4 * j, C)
                if between is not None:
                    between()
                for pair in range(C // 2):
                    for g in range(len(GROUPS)):
                        if g == len(GROUPS) - 1:
                            for m in (2 * pair, 2 * pair + 1):
                                feed(FEED_AFTER[n], m)
                        split_next(at[("down", n, pair, g)].slot)

            def part(name, c):
                act.wait_ge(sig.part_done, at[name].part + c + 1)
                return (at[name].out + c) % 4

            def gates_exp():
                for pair, z in enumerate((u, gate[1])):
                    act.wait_ge(sig.gate_neg, pair + 1)
                    nc.scalar.activation(z[:], z[:], ACT.Exp).then_inc(sig.gate_exp, 1)

            def gates_ln():
                for pair, z in enumerate((u, gate[1])):
                    act.wait_ge(sig.gate_exp, pair + 1)
                    nc.scalar.activation(z[:], z[:], ACT.Ln, bias=1.0).then_inc(sig.gate_ln, 1)

            def decayed_qk(h, meanwhile=None):
                if meanwhile is not None:
                    meanwhile()
                act.wait_ge(sig.diff_ready, h + 1)
                nc.scalar.activation(e[:, 1, :], e[:, 0, :], ACT.Exp, scale=-1.0 / TAU).then_inc(sig.exp_ready, 1)
                nc.scalar.activation(e[:, 0, :], e[:, 0, :], ACT.Exp, scale=1.0 / TAU).then_inc(sig.exp_ready, 1)
                act.wait_ge(sig.qk_scaled, 2 * h + 2)
                if h > 0:
                    act.wait_ge(sig.a_done, h)
                hi_part(qk_hi[:], e[:]).then_inc(sig.qk_hi_ready, 1)
                act.wait_ge(sig.last_diff, h + 1)
                nc.scalar.activation(e[:, 0, :], e[:, 0, :], ACT.Exp, scale=1.0 / TAU).then_inc(sig.last_exp, 1)

            def scores_split(h):
                act.wait_ge(sig.a_done, h + 1)
                hi_part(kst_hi[:], ps[:, 4, :].rearrange("p (t d) -> p t d", t=T)).then_inc(sig.kst_hi_ready, 1)
                act.wait_ge(sig.at_ready, h + 1)
                hi_part(am_hi[:], acc[:].rearrange("p (t d) -> p t d", t=T)).then_inc(sig.at_hi_ready, 1)

            def entering_q(h):
                nc.scalar.activation(e[:, 1, :], b[:, h, :], ACT.Exp, scale=1.0 / TAU).then_inc(sig.in_exp, 1)
                if h > 0:
                    act.wait_ge(sig.s_ready, 7 * h)
                nc.scalar.activation(decay[:], b[:, h, :].rearrange("p (n c) -> p n c", c=CH)[:, :, CH - 1], ACT.Exp,
                                     scale=1.0 / TAU).then_inc(sig.decay_ready, 1)
                act.wait_ge(sig.qin_ready, h + 1)
                hi_part(qin_hi[:], e[:, 1, :]).then_inc(sig.qin_hi_ready, 1)

            def states(h):
                for n in range(NCH - 1):
                    act.wait_ge(sig.s_ready, 7 * h + n + 1)
                    hi_part(S_hi[:, n, :], S[:, n % 2, :]).then_inc(sig.s_hi_ready, 1)

            def values(h, tiles):
                for tt in tiles:
                    bank = part(f"V{h}", tt)
                    hi_part(v_hi[:, h % 2, tt, :], ps[:, bank, 0:DV], scale=rms_tok[:, tt:tt + 1])\
                        .then_inc(sig.v_hi_ready, 1)
                if tiles[-1] == T - 1:
                    split_next(at[f"V{h}"].slot)

            def output_gate(h):
                for c in range(2):
                    act.wait_ge(sig.evacuated, at[f"R{h}"].out + c + 1)
                    nc.scalar.activation(gate[h % 2][:, c, :], gate[h % 2][:, c, :], ACT.Silu)\
                      .then_inc(sig.r_silu, 1)
                split_next(at[f"R{h}"].slot)

            def outputs(h):
                for c in range(2):
                    bank = part(f"c{h}", c)
                    nc.scalar.activation(sq[:, c, :], ps[:, bank, :], ACT.Square).then_inc(sig.o_squared, 1)

            def value_root(h):
                act.wait_ge(sig.o_summed, h + 1)
                nc.scalar.activation(o_rms[:], ps[:, 7, 0:T], ACT.Sqrt, bias=eps[:]).then_inc(sig.o_root, 1)

            def value_split(h):
                act.wait_ge(sig.o_scaled, 2 * h + 2)
                hi_part(o_hi[:, 2 * (h % 2):2 * (h % 2) + 2, :], u[:]).then_inc(sig.o_hi_ready, 1)

            def memory_scale(i):
                act.wait_ge(sig.mem_loaded, 16 * (i + 1))
                junk = (e, t)[i]
                for mt in range(MT):
                    if mt:
                        act.wait_ge(sig.mem_squared, MT * i + mt)
                    nc.scalar.activation(junk[:].rearrange("p a b -> p (a b)"), mem_tok[i][:, mt, :], ACT.Square,
                                         scale=float(D) ** -0.5, accum_out=mem_rms[:, mt:mt + 1])\
                      .then_inc(sig.mem_squared, 1)
                act.wait_ge(sig.mem_squared, MT * (i + 1))
                nc.scalar.activation(mem_rms[:], mem_rms[:], ACT.Sqrt, bias=eps[:]).then_inc(sig.mem_root, 1)
                act.wait_ge(sig.mem_rms_ready, i + 1)
                for mt in range(MT):
                    nc.scalar.activation(mem_tok[i][:, mt, :], mem_tok[i][:, mt, :], ACT.Copy,
                                         scale=mem_rms[:, mt:mt + 1]).then_inc(sig.mem_scaled, 1)

            def memory(i):
                for c in range(C):
                    act.wait_ge(sig.mem_transposed, C * i + c // 2 * 2 + 2)
                    hi_part(mem_norm[i][0][:, c, 0:MEM], ps[:, 4 + c // 2, (c % 2) * MEM:(c % 2 + 1) * MEM],
                            scale=col("n_mem", i * C + c)).then_inc(sig.m_hi_ready, 1)

            def cross_keys(i, pairs):
                for pair in pairs:
                    for c in range(2):
                        bank = part(("xk", i, pair), c)
                        hi_part(xk_hi[:, 2 * pair + c, :], ps[:, bank, 0:MEM]).then_inc(sig.xk_hi_ready, 1)
                    split_next(at[("xk", i, pair)].slot)

            def pool_output(m):
                o = at["pool"].out + m
                act.wait_ge(sig.evacuated, o)
                act.wait_ge(sig.part_done, at["pool"].part + m + 1)
                if m >= 2:
                    act.wait_ge(sig.x_ready, C * X_COUNTED.index(6) + m - 1)
                nc.scalar.activation(t[:, m % 2, :], ps[:, o % 4, :], ACT.Identity, bias=pool_shift[:, m:m + 1],
                                     scale=col("pool_scale", m)).then_inc(sig.evacuated, 1)

            def pooled(g):
                if g < 2:
                    act.wait_ge(sig.mean_ready, g + 1)
                else:
                    act.wait_ge(sig.last_mean, g - 1)
                    act.wait_ge(sig.part_done, at["pool"].part + 2)
                hi_part(p_hi[:, 2 * (g % 3):2 * (g % 3) + 2, :], means[g][:, :, PAD:PAD + SEQ])\
                    .then_inc(sig.p_hi_ready, 1)

            def softmax(i, h):
                n = HEADS * i + h
                act.wait_ge(sig.neg_max_ready, n + 1)
                for tt in range(T):
                    nc.scalar.activation(p_tok[:, h, tt, :],
                                         ps[:, 4 + 2 * (h % 2) + tt // 2, (tt % 2) * MEM:(tt % 2 + 1) * MEM],
                                         ACT.Exp, bias=sbias[:, tt:tt + 1], scale=rms_tok[:, tt:tt + 1],
                                         accum_out=ssum[:, tt:tt + 1]).then_inc(sig.exp_done, 1)

            def p_split(i, h):
                n = HEADS * i + h
                act.wait_ge(sig.p_transposed, n + 1)
                if h >= 2:
                    act.wait_ge(sig.part_done, at[("pv", i, h - 2)].part + 2)
                hi_part(probs_T[h % 2][0][:], ps[:, 4 + 2 * (h % 2):6 + 2 * (h % 2), :])\
                    .then_inc(sig.pT_hi_ready, 1)

            def cross_values(i, h):
                for mt in range(MT):
                    bank = part(("xv", i, h), mt)
                    hi_part(xv_hi[:, mt, h * DH:(h + 1) * DH], ps[:, bank, 0:COLS]).then_inc(sig.xv_hi_ready, 1)
                split_next(at[("xv", i, h)].slot)

            def cross_outputs(i, h):
                for c in range(2):
                    bank = part(("pv", i, h), c)
                    hi_part(xo_hi[:, 2 * h + c, :], ps[:, bank, :]).then_inc(sig.xo_hi_ready, 1)

            def out_pair(i, pair, f):
                for m in (2 * pair, 2 * pair + 1):
                    if m % 2 == 1 and pair < 3:
                        split_next(at[("OUT", i, pair)].slot)
                    if f is not None:
                        feed(f, m)
                if pair == 3:
                    split_next(at[("OUT", i, pair)].slot)

            def cross_query(i, h):
                for c in range(2):
                    if c == 1 and h >= 1:
                        softmax(i, h - 1)
                        if (i, h) == (1, 3):
                            p_split(1, 1)
                    bank = part(("xq", i, h), c)
                    if h >= 2 and c == 0:
                        act.wait_ge(sig.scores_done, HEADS * i + h - 1)
                    hi_part(xq_hi[:, 2 * (h % 2) + c, :], ps[:, bank, :]).then_inc(sig.xq_hi_ready, 1)
                if (i, h) != (1, 3):
                    split_next(at[("xq", i, h)].slot)

            def cross(i):
                cross_query(i, 0)
                norm_roots(4 * i + 2)
                cross_query(i, 1)
                cross_query(i, 2)
                if i == 0:
                    cross_query(0, 3)
                    cross_values(0, 0)
                    softmax(0, 3)
                    p_split(0, 0)
                    cross_values(0, 1)
                    p_split(0, 1)
                    cross_outputs(0, 0)
                    p_split(0, 2)
                    cross_values(0, 2)
                    cross_outputs(0, 1)
                    p_split(0, 3)
                    cross_values(0, 3)
                    cross_outputs(0, 2)
                    cross_outputs(0, 3)
                else:
                    p_split(1, 0)
                    cross_query(1, 3)
                    p_split(1, 2)
                    softmax(1, 3)
                    cross_outputs(1, 0)
                    p_split(1, 3)
                    cross_outputs(1, 1)
                    split_next(at[("xq", 1, 3)].slot)
                    cross_outputs(1, 2)
                    cross_outputs(1, 3)
                for pair in range(4):
                    for m in (2 * pair, 2 * pair + 1):
                        feed(4 * i + 3, m)
                    split_next(at[("xo", i, pair)].slot)

            act.dma_start(first_rows[0:2 * C, :], rows[0]).then_inc(sig.first_loaded, 16)
            act.wait_ge(sig.consts_ready, 5)
            load_silu()
            act.wait_ge(sig.cols_ready, 1)
            for m in range(C):
                feed(0, m)
                if m == 2:
                    split_hi(0, 16, None, C)
            split_hi(1, 16, None, C)
            ffn(0)
            norm_roots(1)
            act.wait_ge(sig.gates_loaded, 32)
            hi_part(g1_hi[:], g1[:]).then_inc(sig.g_hi_ready, 1)
            hi_part(g2_hi[:], g2[:]).then_inc(sig.g_hi_ready, 1)
            split_next(at["Q0"].slot)
            act.wait_ge(sig.gt_ready, 1)
            hi_part(gt_hi[:], gt[:]).then_inc(sig.gt_hi_ready, 1)
            split_next(at["K0"].slot)
            gates_exp()
            values(0, (0, 1))
            gates_ln()
            decayed_qk(0, lambda: values(0, (2, 3)))
            scores_split(0)
            output_gate(0)
            entering_q(0)
            values(1, (0, 1))
            states(0)
            decayed_qk(1, lambda: values(1, (2, 3)))
            output_gate(1)
            outputs(0)
            entering_q(1)
            scores_split(1)
            value_root(0)
            split_next(at["Q1"].slot)
            value_split(0)
            states(1)
            split_next(at["K1"].slot)
            decayed_qk(2, lambda: values(2, (0, 1)))
            values(2, (2, 3))
            outputs(1)
            entering_q(2)
            scores_split(2)
            value_root(1)
            output_gate(2)
            value_split(1)
            values(3, (0, 1))
            states(2)
            decayed_qk(3, lambda: values(3, (2, 3)))
            out_pair(0, 0, None)
            outputs(2)
            entering_q(3)
            out_pair(0, 1, None)
            scores_split(3)
            value_root(2)
            out_pair(0, 2, None)
            states(3)
            memory_scale(0)
            out_pair(0, 3, None)
            value_split(2)
            output_gate(3)
            memory(0)
            outputs(3)
            cross_keys(0, (0,))
            value_root(3)
            cross_keys(0, (1, 2))
            value_split(3)
            cross_keys(0, (3,))
            for pair in range(4):
                out_pair(1, pair, 2)
            cross(0)
            ffn(1)
            memory_scale(1)
            ffn(2, between=lambda: memory(1))
            cross_keys(1, (0,))
            norm_roots(5)
            for m in range(4, C):
                hi_part(up[:, m, PAD:], x[:, m, :], scale=gain(5, m)).then_inc(sig.up_gained, 1)
            cross_keys(1, (1, 2))
            pooled(0)
            cross_keys(1, (3,))
            cross_values(1, 0)
            pooled(1)
            for h in range(1, 4):
                cross_values(1, h)
            pooled(2)
            act.wait_ge(sig.shift_ready, 1)
            pool_output(0)
            for m in range(C):
                if m + 1 < C:
                    pool_output(m + 1)
                if m == 0:
                    pooled(3)
                feed(6, m)
            split_next(at["pool"].slot)
            cross(1)
            ffn(3)
            norm_roots(LAST)
            for piece in range(1, 2 * T, 2):
                tile, half = piece % T, piece // T
                act.wait_ge(sig.y_transposed, piece + 1)
                act.wait_ge(sig.tok_ready, len(TOK_FEEDS))
                nc.scalar.activation(y_tok[:, tile, half * 512:(half + 1) * 512], ps[:, OUT_BANK[piece], :], ACT.Copy,
                                     scale=rms_tok[:, tile:tile + 1]).then_inc(sig.y_out_by_act, 1)

        @block.vector
        def _(dve):
            def lo_part(out_ap, value, hi):
                return nc.vector.tensor_tensor(out_ap, value, hi.bitcast(F32), ALU.subtract)

            def scaled_lo_part(out_ap, value, scale, hi):
                return nc.vector.scalar_tensor_tensor(out_ap, value, scale, hi.bitcast(F32), ALU.mult, ALU.subtract)

            def split_lo(s, hi_count, nrows):
                dve.wait_ge(sig.w_hi_ready, hi_count)
                lo_part(w_lo[:, s, 0:nrows, :], raw[:, s, 0:nrows, :], w_hi[:, s, 0:nrows, :])\
                    .then_inc(sig.w_lo_ready, 1)

            def split_next(w):
                if w + 2 < SLOTS:
                    split_lo(w % 2, w + 3, slot_rows[w + 2])

            def part(name, c):
                dve.wait_ge(sig.part_done, at[name].part + c + 1)
                return (at[name].out + c) % 4

            def feed(f, m):
                if f == LAST:
                    dve.wait_ge(sig.sq_ready, C * f + m + 1)
                    dve.wait_ge(*x_final(f, m))
                    nc.vector.tensor_scalar_mul(x[:, m, :], x[:, m, :], gain(f, m)).then_inc(sig.y_ready, 1)
                elif f in H_BASE:
                    dve.wait_ge(sig.h_hi_ready, H_BASE[f] + m + 1)
                    scaled_lo_part(h_lo[:, m, :], x[:, m, :], gain(f, m), h_hi[:, m, :]).then_inc(sig.h_ready, 1)

            def norm_inverses(f):
                if f in SUM_FEEDS:
                    dve.wait_ge(sig.norm_root, SUM_FEEDS.index(f) + 1)
                    nc.vector.reciprocal(rms[:], rms[:]).then_inc(sig.norm_ready, 1)
                if f in TOK_FEEDS:
                    n = TOK_FEEDS.index(f) + 1
                    dve.wait_ge(sig.tok_root, n)
                    if f in (2, 6):
                        nc.vector.reciprocal(rms_tok[:], rms_tok[:]).then_inc(sig.tok_inverse, 1)
                        dve.wait_ge(sig.tok_inverse, f // 6 + 1)
                        nc.vector.tensor_scalar_mul(rms_tok[:], rms_tok[:], float(DH) ** -0.5)\
                          .then_inc(sig.tok_ready, 1)
                    else:
                        nc.vector.reciprocal(rms_tok[:], rms_tok[:]).then_inc(sig.tok_ready, 1)
                if f in SUM_FEEDS:
                    dve.wait_ge(sig.norm_ready, RMS_FEEDS.index(f) + 1)
                if f in TOK_FEEDS:
                    dve.wait_ge(sig.tok_ready, n)

            def spread_rms(f):
                dve.wait_ge(sig.rms_spread, SPREAD_FEEDS.index(f) + 1)
                nc.vector.tensor_copy(rms[:], ps[:, 4, :]).then_inc(sig.norm_ready, 1)
                dve.wait_ge(sig.norm_ready, RMS_FEEDS.index(f) + 1)

            def ffn(n, between=None):
                norm_inverses((0, 3, 4, 7)[n])
                w0, p0 = at[("gu", n, 0)].slot, at[("gu", n, 0)].part
                o0 = at[("gu", n, 0)].out
                with dve.Fori(0, FC // 2) as j:
                    for c in range(2):
                        dve.wait_ge(sig.part_done, p0 + c + 1 + 4 * j)
                        nc.vector.tensor_tensor(t[:, c, :], ps[:, (o0 + c) % 4, :], rms[:], ALU.mult)\
                          .then_inc(sig.evacuated, 1)
                    split_lo(w0 % 2, w0 + 3 + 2 * j, C)
                    for c in range(2):
                        dve.wait_ge(sig.part_done, p0 + c + 3 + 4 * j)
                        dve.wait_ge(sig.silu_done, FC * n + c + 1 + 2 * j)
                        nc.vector.tensor_tensor(t[:, c, :], t[:, c, :], ps[:, (o0 + 2 + c) % 4, :], ALU.mult)\
                          .then_inc(sig.evacuated, 1)
                    for c in range(2):
                        dve.wait_ge(sig.mid_hi_ready, FC * n + c + 1 + 2 * j)
                        lo_part(mid_lo[:, 2 * j + c, :], t[:, c, :], mid_hi[:, 2 * j + c, :]).then_inc(sig.mid_ready, 1)
                    split_lo((w0 + 1) % 2, w0 + 4 + 2 * j, C)
                    dve.wait_ge(sig.mid_ready, FC * n + 2 + 2 * j)
                if between is not None:
                    between()
                for pair in range(C // 2):
                    for g in range(len(GROUPS)):
                        name = ("down", n, pair, g)
                        if g == len(GROUPS) - 1:
                            for c in range(2):
                                m, o = 2 * pair + c, at[name].out + c
                                bank = part(name, c)
                                nc.vector.scalar_tensor_tensor(t[:, c, :], ps[:, bank, :], 0.5, rms[:], ALU.mult,
                                                               ALU.mult).then_inc(sig.evacuated, 1)
                                dve.wait_ge(sig.evacuated, o + 1)
                                nc.vector.tensor_tensor(x[:, m, :], x[:, m, :], t[:, c, :], ALU.add)\
                                  .then_inc(sig.x_ready, 1)
                                feed(FEED_AFTER[n], m)
                        split_next(at[name].slot)

            def plain_residual(name, f, m):
                bank = part(name, m % 2)
                nc.vector.tensor_tensor(x[:, m, :], ps[:, bank, :], x[:, m, :], ALU.add).then_inc(sig.evacuated, 1)
                if f is not None:
                    feed(f, m)

            def gates_negative(pair):
                hs = slice(2 * pair, 2 * pair + 2)
                dve.wait_ge(sig.z_biased, 2 * pair + 2)
                nc.vector.scalar_tensor_tensor((u, gate[1])[pair][:], b[:, hs, :], -1.0, b[:, hs, :],
                                               ALU.mult, ALU.min)\
                  .then_inc(sig.gate_neg, 1)

            def gates_sum(pair):
                hs, ln = slice(2 * pair, 2 * pair + 2), (u, gate[1])[pair]
                dve.wait_ge(sig.gate_ln, pair + 1)
                nc.vector.scalar_tensor_tensor(ln[:], b[:, hs, :], 0.0, ln[:], ALU.min, ALU.subtract)\
                  .then_inc(sig.gate_log, 1)
                dve.wait_ge(sig.gate_log, pair + 1)
                dve.wait_ge(sig.scanmask_ready, 2)
                for c in range(2):
                    nc.vector.tensor_tensor_scan(b[:, 2 * pair + c, :], acc[:], ln[:, c, :], 0.0, ALU.mult, ALU.add)\
                      .then_inc(sig.b_ready, 1)
                dve.wait_ge(sig.b_ready, 2 * pair + 2)

            def by_chunk(ap):
                return ap.rearrange("p (n c) -> p n c", c=CH)

            def decayed_qk(h, meanwhile=None):
                bc = by_chunk(b[:, h, :])
                if h > 0:
                    dve.wait_ge(sig.qin_lo_ready, h)
                nc.vector.tensor_tensor(by_chunk(e[:, 0, :]), bc,
                                        bc[:, :, CH // 2 - 1:CH // 2].broadcast_to([P, NCH, CH]),
                                        ALU.subtract).then_inc(sig.diff_ready, 1)
                if meanwhile is not None:
                    meanwhile()
                dve.wait_ge(sig.exp_ready, 2 * h + 2)
                nc.vector.tensor_tensor(e[:, 0, :], q[:, h % 2, :], e[:, 0, :], ALU.mult).then_inc(sig.qk_scaled, 1)
                nc.vector.tensor_tensor(e[:, 1, :], k[:, h % 2, :], e[:, 1, :], ALU.mult).then_inc(sig.qk_scaled, 1)
                dve.wait_ge(sig.qk_hi_ready, h + 1)
                dve.wait_ge(sig.qk_scaled, 2 * h + 2)
                lo_part(qk_lo[:], e[:], qk_hi[:]).then_inc(sig.qk_lo_ready, 1)
                dve.wait_ge(sig.qk_lo_ready, h + 1)
                nc.vector.tensor_tensor(by_chunk(e[:, 0, :]), bc[:, :, CH - 1:CH].broadcast_to([P, NCH, CH]), bc,
                                        ALU.subtract).then_inc(sig.last_diff, 1)
                dve.wait_ge(sig.last_exp, h + 1)
                nc.vector.tensor_tensor(k[:, h % 2, :], k[:, h % 2, :], e[:, 0, :], ALU.mult).then_inc(sig.kst_ready, 1)

            def scores_split(h):
                dve.wait_ge(sig.kst_hi_ready, h + 1)
                lo_part(kst_lo[:], ps[:, 4, :].rearrange("p (t d) -> p t d", t=T), kst_hi[:])\
                    .then_inc(sig.kst_lo_ready, 1)
                masked = acc[:].rearrange("p (t d) -> p t d", t=T)
                if h == 0:
                    nc.vector.memset(acc[:], 0.0).then_inc(sig.at_zeroed, 1)
                    dve.wait_ge(sig.at_zeroed, 1)
                    dve.wait_ge(sig.mask_ready, 2)
                else:
                    dve.wait_ge(sig.at_lo_ready, h)
                nc.vector.copy_predicated(masked, mask[:].bitcast(I32).unsqueeze(1).broadcast_to([P, T, P]),
                                          ps[:, 5, :].rearrange("p (t d) -> p t d", t=T)).then_inc(sig.at_ready, 1)
                dve.wait_ge(sig.at_hi_ready, h + 1)
                lo_part(am_lo[:], masked, am_hi[:]).then_inc(sig.at_lo_ready, 1)

            def entering_q(h):
                dve.wait_ge(sig.in_exp, h + 1)
                nc.vector.tensor_tensor(e[:, 1, :], q[:, h % 2, :], e[:, 1, :], ALU.mult).then_inc(sig.qin_ready, 1)
                dve.wait_ge(sig.qin_hi_ready, h + 1)
                lo_part(qin_lo[:], e[:, 1, :], qin_hi[:]).then_inc(sig.qin_lo_ready, 1)

            def states(h):
                dve.wait_ge(sig.decay_ready, h + 1)
                for n in range(NCH - 1):
                    half, tt = n % 2, n // 2
                    update = ps[:, 4 + 2 * half + tt // 2, (tt % 2) * DV:(tt % 2 + 1) * DV]
                    if n >= 2 or (h > 0 and n == 0):
                        dve.wait_ge(sig.s_lo_ready, 7 * h + max(n - 1, 0))
                    dve.wait_ge(sig.kv_done, 7 * h + UPDATES_BEFORE[n])
                    if n == 0:
                        nc.vector.tensor_copy(S[:, 0, :], update).then_inc(sig.s_ready, 1)
                    else:
                        dve.wait_ge(sig.s_ready, 7 * h + n)
                        nc.vector.scalar_tensor_tensor(S[:, n % 2, :], S[:, (n - 1) % 2, :], decay[:, n:n + 1], update,
                                                       ALU.mult, ALU.add).then_inc(sig.s_ready, 1)
                    dve.wait_ge(sig.s_hi_ready, 7 * h + n + 1)
                    dve.wait_ge(sig.s_ready, 7 * h + n + 1)
                    lo_part(S_lo[:, n, :], S[:, n % 2, :], S_hi[:, n, :]).then_inc(sig.s_lo_ready, 1)

            def values(h, tiles):
                for tt in tiles:
                    bank = part(f"V{h}", tt)
                    dve.wait_ge(sig.v_hi_ready, T * h + tt + 1)
                    scaled_lo_part(v_lo[:, h % 2, tt, :], ps[:, bank, 0:DV], rms_tok[:, tt:tt + 1],
                                   v_hi[:, h % 2, tt, :])\
                        .then_inc(sig.evacuated, 1)
                if tiles[-1] == T - 1:
                    split_next(at[f"V{h}"].slot)

            def output_gate(h):
                if h >= 2:
                    dve.wait_ge(sig.evacuated, at[f"c{h - 2}"].out + 2)
                for c in range(2):
                    bank = part(f"R{h}", c)
                    nc.vector.tensor_tensor(gate[h % 2][:, c, :], ps[:, bank, :], rms[:], ALU.mult)\
                      .then_inc(sig.evacuated, 1)
                split_next(at[f"R{h}"].slot)

            def outputs(h):
                if h > 0:
                    dve.wait_ge(sig.o_lo_ready, h)
                for c in range(2):
                    bank = part(f"c{h}", c)
                    dve.wait_ge(sig.o_squared, 2 * h + c + 1)
                    dve.wait_ge(sig.r_silu, 2 * h + c + 1)
                    nc.vector.scalar_tensor_tensor(u[:, c, :], ps[:, bank, :], col("gla_onorm", c),
                                                   gate[h % 2][:, c, :],
                                                   ALU.mult, ALU.mult).then_inc(sig.evacuated, 1)

            def value_inverse(h):
                dve.wait_ge(sig.o_root, h + 1)
                nc.vector.reciprocal(o_rms[:], o_rms[:]).then_inc(sig.o_rms, 1)

            def value_scale(h):
                dve.wait_ge(sig.evacuated, at[f"c{h}"].out + 2)
                dve.wait_ge(sig.o_spread, h + 1)
                for c in range(2):
                    nc.vector.tensor_tensor(u[:, c, :], u[:, c, :], ps[:, 7, :], ALU.mult).then_inc(sig.o_scaled, 1)

            def value_split(h):
                dve.wait_ge(sig.o_scaled, 2 * h + 2)
                dve.wait_ge(sig.o_hi_ready, h + 1)
                hs = slice(2 * (h % 2), 2 * (h % 2) + 2)
                lo_part(o_lo[:, hs, :], u[:], o_hi[:, hs, :]).then_inc(sig.o_lo_ready, 1)

            def query_key(name, to, factor):
                for c in range(2):
                    bank = part(name, c)
                    nc.vector.scalar_tensor_tensor(to[:, c, :], ps[:, bank, :], factor, rms[:], ALU.mult, ALU.mult)\
                      .then_inc(sig.evacuated, 1)
                split_next(at[name].slot)
                dve.wait_ge(sig.evacuated, at[name].out + 2)

            def memory_scale(i):
                dve.wait_ge(sig.mem_root, i + 1)
                nc.vector.reciprocal(mem_rms[:], mem_rms[:]).then_inc(sig.mem_rms_ready, 1)

            def memory(i):
                for c in range(C):
                    dve.wait_ge(sig.m_hi_ready, C * i + c // 2 * 2 + 2)
                    scaled_lo_part(mem_norm[i][1][:, c, 0:MEM], ps[:, 4 + c // 2, (c % 2) * MEM:(c % 2 + 1) * MEM],
                                   col("n_mem", i * C + c), mem_norm[i][0][:, c, 0:MEM]).then_inc(sig.m_lo_ready, 1)

            def evacuate_split(name, c, n, hi_sem, hi_count, lo, hi):
                bank = part(name, c)
                dve.wait_ge(hi_sem, hi_count)
                lo_part(lo, ps[:, bank, 0:n], hi).then_inc(sig.evacuated, 1)

            def cross_keys(i, pairs):
                for pair in pairs:
                    for c in range(2):
                        kk = 2 * pair + c
                        evacuate_split(("xk", i, pair), c, MEM, sig.xk_hi_ready, C * i + kk + 1, xk_lo[:, kk, :],
                                       xk_hi[:, kk, :])
                    split_next(at[("xk", i, pair)].slot)

            def softmax_max(i, h):
                n = HEADS * i + h
                dve.wait_ge(sig.scores_done, n + 1)
                bank = 4 + 2 * (h % 2)
                nc.vector.reduce_max(smax[:], ps[:, bank:bank + 2, :].rearrange("p b (h m) -> p (b h) m", m=MEM),
                                     AX_X).then_inc(sig.max_ready, 1)
                dve.wait_ge(sig.max_ready, n + 1)
                nc.vector.scalar_tensor_tensor(sbias[:], smax[:], -1.0, rms_tok[:], ALU.mult, ALU.mult)\
                  .then_inc(sig.neg_max_ready, 1)

            def softmax_divide(i, h):
                n = HEADS * i + h
                dve.wait_ge(sig.exp_done, T * (n + 1))
                nc.vector.reciprocal(ssum[:], ssum[:]).then_inc(sig.sum_inverted, 1)
                dve.wait_ge(sig.sum_inverted, n + 1)
                for tt in range(T):
                    last = nc.vector.tensor_scalar_mul(p_tok[:, h, tt, :], p_tok[:, h, tt, :], ssum[:, tt:tt + 1])
                last.then_inc(sig.p_ready, 1)

            def p_split(i, h):
                n = HEADS * i + h
                dve.wait_ge(sig.pT_hi_ready, n + 1)
                lo_part(probs_T[h % 2][1][:], ps[:, 4 + 2 * (h % 2):6 + 2 * (h % 2), :], probs_T[h % 2][0][:])\
                    .then_inc(sig.pT_lo_ready, 1)

            def cross_values(i, h):
                vs = slice(h * DH, (h + 1) * DH)
                for mt in range(MT):
                    evacuate_split(("xv", i, h), mt, COLS, sig.xv_hi_ready, MT * (HEADS * i + h) + mt + 1,
                                   xv_lo[:, mt, vs], xv_hi[:, mt, vs])
                split_next(at[("xv", i, h)].slot)

            def cross_outputs(i, h):
                for c in range(2):
                    evacuate_split(("pv", i, h), c, SEQ, sig.xo_hi_ready, C * i + 2 * h + c + 1, xo_lo[:, 2 * h + c, :],
                                   xo_hi[:, 2 * h + c, :])

            def out_pair(i, pair, f):
                for m in (2 * pair, 2 * pair + 1):
                    if m % 2 == 1 and pair < 3:
                        split_next(at[("OUT", i, pair)].slot)
                    plain_residual(("OUT", i, pair), f, m)
                if pair == 3:
                    split_next(at[("OUT", i, pair)].slot)

            def softmax(i, h):
                softmax_max(i, h)
                softmax_divide(i, h)

            def cross_query(i, h):
                for c in range(2):
                    if c == 1 and h >= 1:
                        softmax(i, h - 1)
                        if (i, h) == (1, 3):
                            p_split(1, 1)
                    at_q = 2 * (h % 2) + c
                    evacuate_split(("xq", i, h), c, SEQ, sig.xq_hi_ready, C * i + 2 * h + c + 1,
                                   xq_lo[:, at_q, :], xq_hi[:, at_q, :])
                if (i, h) != (1, 3):
                    split_next(at[("xq", i, h)].slot)

            def cross(i):
                cross_query(i, 0)
                norm_inverses(4 * i + 2)
                cross_query(i, 1)
                cross_query(i, 2)
                if i == 0:
                    cross_query(0, 3)
                    cross_values(0, 0)
                    softmax(0, 3)
                    p_split(0, 0)
                    cross_values(0, 1)
                    p_split(0, 1)
                    cross_outputs(0, 0)
                    p_split(0, 2)
                    cross_values(0, 2)
                    cross_outputs(0, 1)
                    p_split(0, 3)
                    cross_values(0, 3)
                    cross_outputs(0, 2)
                    cross_outputs(0, 3)
                else:
                    p_split(1, 0)
                    cross_query(1, 3)
                    p_split(1, 2)
                    softmax(1, 3)
                    cross_outputs(1, 0)
                    p_split(1, 3)
                    cross_outputs(1, 1)
                    split_next(at[("xq", 1, 3)].slot)
                    cross_outputs(1, 2)
                    cross_outputs(1, 3)
                for pair in range(4):
                    for m in (2 * pair, 2 * pair + 1):
                        plain_residual(("xo", i, pair), 4 * i + 3, m)
                    split_next(at[("xo", i, pair)].slot)

            def windows(g):
                w = WINDOWS[g]
                buf = g % 2
                steps = []
                step = 1
                while step < w:
                    steps.append(step)
                    step *= 2
                src = up[:, 2 * g:2 * g + 2, :]
                for n, step in enumerate(steps):
                    dst = sums[:, (buf + len(steps) - 1 - n) % 2]
                    if g > 0:
                        dve.wait_ge(sig.p_lo_ready, g)
                    nc.vector.tensor_tensor(dst[:, :, PAD:], src[:, :, PAD:], src[:, :, PAD - step:PAD + SEQ - step],
                                            ALU.add).then_inc(sig.window_ready, 1)
                    window_count[0] += 1
                    dve.wait_ge(sig.window_ready, window_count[0])
                    src = dst

            def pooled_mean(g):
                w, src = WINDOWS[g], means[g]
                head, body = slice(PAD, 2 * PAD), slice(2 * PAD, PAD + SEQ)
                for c in range(2):
                    nc.vector.tensor_tensor(src[:, c, head], src[:, c, head], inv_count[:, g, :], ALU.mult)\
                      .then_inc(sig.window_ready, 1)
                window_count[0] += 2
                dve.wait_ge(sig.window_ready, window_count[0])
                nc.vector.tensor_tensor(src[:, :, head], src[:, :, head], up[:, 2 * g:2 * g + 2, head], ALU.subtract)\
                  .then_inc(sig.window_ready, 1)
                window_count[0] += 1
                dve.wait_ge(sig.window_ready, window_count[0])
                nc.vector.scalar_tensor_tensor(src[:, :, body], src[:, :, body], 1.0 / w, up[:, 2 * g:2 * g + 2, body],
                                               ALU.mult, ALU.subtract).then_inc(sig.mean_ready, 1)
                pooled_lo(g)

            def pooled_lo(g):
                dve.wait_ge(sig.p_hi_ready, g + 1)
                if g < 2:
                    dve.wait_ge(sig.mean_ready, g + 1)
                else:
                    dve.wait_ge(sig.last_mean, g - 1)
                gs = slice(2 * (g % 3), 2 * (g % 3) + 2)
                lo_part(p_lo[:, gs, :], means[g][:, :, PAD:], p_hi[:, gs, :]).then_inc(sig.p_lo_ready, 1)

            def pool_output(m):
                dve.wait_ge(sig.evacuated, at["pool"].out + m + 1)
                nc.vector.tensor_tensor(x[:, m, :], x[:, m, :], t[:, m % 2, :], ALU.add).then_inc(sig.x_ready, 1)

            def all_columns():
                dve.wait_ge(sig.cols_done, 1)
                nc.vector.tensor_copy(cols[:, 2 * C:], ps[:, 7, 2 * C:NR]).then_inc(sig.cols_ready, 1)
                dve.wait_ge(sig.cols_ready, 2)
                first_b, first_scale = at_row["pool_b"], at_row["pool_scale"]
                nc.vector.tensor_tensor(pool_shift[:], cols[:, first_b:first_b + C],
                                        cols[:, first_scale:first_scale + C],
                                        ALU.mult).then_inc(sig.shift_ready, 1)

            for m in range(C):
                bank = part(("in", m), 0)
                nc.vector.tensor_copy(x[:, m, :], ps[:, bank, :]).then_inc(sig.evacuated, 1)
                if m == 0:
                    dve.wait_ge(sig.first_cols_done, 1)
                    nc.vector.tensor_copy(cols[:, 0:2 * C], ps[:, 7, 0:2 * C]).then_inc(sig.cols_ready, 1)
                    dve.wait_ge(sig.cols_ready, 1)
                else:
                    feed(0, m - 1)
                if m == 3:
                    split_lo(0, 1, C)
            feed(0, C - 1)
            split_lo(1, 2, C)
            ffn(0, between=all_columns)
            norm_inverses(1)
            for n, (lo, value, hi) in enumerate(((g1_lo, g1, g1_hi), (g2_lo, g2, g2_hi))):
                dve.wait_ge(sig.g_hi_ready, n + 1)
                lo_part(lo[:], value[:], hi[:]).then_inc(sig.g_lo_ready, 1)
            spread_rms(1)
            query_key("Q0", q, float(DK) ** -0.5)
            dve.wait_ge(sig.g1_done, 1)
            nc.vector.tensor_tensor(gt[:], ps[0:RANK, 6, :], rms[0:RANK, :], ALU.mult).then_inc(sig.gt_ready, 1)
            dve.wait_ge(sig.gt_ready, 1)
            dve.wait_ge(sig.gt_hi_ready, 1)
            lo_part(gt_lo[:], gt[:], gt_hi[:]).then_inc(sig.gt_lo_ready, 1)
            query_key("K0", k, 1.0)
            for pair in range(2):
                for h in (2 * pair, 2 * pair + 1):
                    dve.wait_ge(sig.z_done, h + 1)
                    nc.vector.tensor_scalar_add(b[:, h, :], ps[:, 4 + h, :], col("gla_b_g", h))\
                      .then_inc(sig.z_biased, 1)
                gates_negative(pair)
            values(0, (0, 1))
            gates_sum(0)
            decayed_qk(0, lambda: values(0, (2, 3)))
            gates_sum(1)
            scores_split(0)
            output_gate(0)
            entering_q(0)
            values(1, (0, 1))
            states(0)
            decayed_qk(1, lambda: values(1, (2, 3)))
            output_gate(1)
            outputs(0)
            entering_q(1)
            scores_split(1)
            value_inverse(0)
            query_key("Q1", q, float(DK) ** -0.5)
            value_scale(0)
            value_split(0)
            states(1)
            query_key("K1", k, 1.0)
            decayed_qk(2, lambda: values(2, (0, 1)))
            values(2, (2, 3))
            outputs(1)
            entering_q(2)
            scores_split(2)
            value_inverse(1)
            output_gate(2)
            value_scale(1)
            value_split(1)
            values(3, (0, 1))
            states(2)
            decayed_qk(3, lambda: values(3, (2, 3)))
            out_pair(0, 0, None)
            outputs(2)
            entering_q(3)
            out_pair(0, 1, None)
            scores_split(3)
            value_inverse(2)
            for m in (4, 5):
                plain_residual(("OUT", 0, 2), None, m)
            value_scale(2)
            split_next(at[("OUT", 0, 2)].slot)
            states(3)
            memory_scale(0)
            out_pair(0, 3, None)
            value_split(2)
            output_gate(3)
            memory(0)
            outputs(3)
            cross_keys(0, (0,))
            value_inverse(3)
            cross_keys(0, (1, 2))
            value_scale(3)
            value_split(3)
            cross_keys(0, (3,))
            for pair in range(4):
                out_pair(1, pair, 2)
            cross(0)
            nc.vector.memset(inv_count[:, 0, :], 1.0).then_inc(sig.counts_ready, 1)
            dve.wait_ge(sig.counts_ready, 1)
            nc.vector.tensor_tensor_scan(inv_count[:, 3, :], inv_count[:, 0, :], inv_count[:, 0, :], 0.0, ALU.mult,
                                         ALU.add).then_inc(sig.counts_ready, 1)
            dve.wait_ge(sig.counts_ready, 2)
            for g in range(4):
                nc.vector.tensor_scalar_min(inv_count[:, g, :], inv_count[:, 3, :], float(WINDOWS[g]))\
                  .then_inc(sig.counts_ready, 1)
            dve.wait_ge(sig.counts_ready, 6)
            nc.vector.reciprocal(inv_count[:], inv_count[:]).then_inc(sig.counts_ready, 1)
            ffn(1)
            memory_scale(1)
            ffn(2, between=lambda: memory(1))
            nc.vector.memset(up[:, :, 0:PAD], 0.0).then_inc(sig.pads_zeroed, 1)
            for buf in range(2):
                nc.vector.memset(sums[:, buf, :, 0:PAD], 0.0).then_inc(sig.pads_zeroed, 1)
            cross_keys(1, (0,))
            norm_inverses(5)
            cross_keys(1, (1,))
            spread_rms(5)
            dve.wait_ge(sig.counts_ready, 7)
            dve.wait_ge(sig.pads_zeroed, 3)
            for m in range(4):
                nc.vector.scalar_tensor_tensor(up[:, m, PAD:], x[:, m, :], gain(5, m), rms[:], ALU.mult, ALU.mult)\
                  .then_inc(sig.up_ready, 1)
            dve.wait_ge(sig.up_ready, 4)
            window_count = [0]
            cross_keys(1, (2,))
            windows(0)
            pooled_mean(0)
            cross_keys(1, (3,))
            windows(1)
            cross_values(1, 0)
            pooled_mean(1)
            for h in range(1, 4):
                cross_values(1, h)
            pooled_lo(2)
            for m in range(C):
                pool_output(m)
                if m == 1:
                    pooled_lo(3)
                if m >= 1:
                    feed(6, m - 1)
            feed(6, C - 1)
            split_next(at["pool"].slot)
            cross(1)
            ffn(3)
            norm_inverses(LAST)
            for piece in range(0, 2 * T, 2):
                tile, half = piece % T, piece // T
                dve.wait_ge(sig.y_transposed, piece + 1)
                nc.vector.tensor_scalar_mul(y_tok[:, tile, half * 512:(half + 1) * 512], ps[:, OUT_BANK[piece], :],
                                            rms_tok[:, tile:tile + 1]).then_inc(sig.y_out_by_dve, 1)


def kernel(**inputs):
    import numpy as np
    import concourse.bacc as bacc
    from concourse.bass_utils import run_bass_kernel_spmd

    nc = bacc.Bacc("TRN2", target_bir_lowering=False, num_devices=1)
    arrays, io = {}, {}
    for name, value in inputs.items():
        array = np.ascontiguousarray(value)
        arrays[f"in_{name}"] = array
        io[name] = nc.dram_tensor(f"in_{name}", array.shape, mybir.dt.from_np(array.dtype), kind="ExternalInput").ap()
    shape = arrays["in_x"].shape
    out = nc.dram_tensor("out", shape, F32, kind="ExternalOutput").ap()
    trunk(nc, namedtuple("Inputs", io)(**io), out)
    result = run_bass_kernel_spmd(nc, [arrays], core_ids=[0])
    return result.results[0]["out"]
```
